# Optimizing a Trainium2 kernel written in Bass

```python
import jax, jax.numpy as jnp
from jax import lax
import numpy as np

D_MODEL = 1024
BATCH = 1
SEQ = 512
DEPTH = 2

N_A_LAYERS = DEPTH // 2
CONV_WIDTH = 3
PATTERNS = ((128, 1), (512, 4), (2048, 16))
N_GROUPS = len(PATTERNS)
H_G = 8
HEAD_DIM = 64
D_FF = 4 * D_MODEL
EPS = 1e-5
ALIBI_MAX_BIAS = 8.0
NEG_INF = -1e30

kernel_name = 'yoco_shortconv_dilated_attn_trunk'

def rmsnorm(x, g):
    xf = x.astype(jnp.float32)
    y = xf * lax.rsqrt(jnp.mean(xf * xf, axis=-1, keepdims=True) + EPS)
    return (y * g.astype(jnp.float32)).astype(x.dtype)

def short_conv_mixer(h, w_in, conv_w, w_out):
    S = h.shape[1]
    b, c, u = jnp.split(h @ w_in, 3, axis=-1)
    up = jnp.pad(c * u, ((0, 0), (CONV_WIDTH - 1, 0), (0, 0)))
    conv = sum(conv_w[k] * up[:, CONV_WIDTH - 1 - k: CONV_WIDTH - 1 - k + S] for k in range(CONV_WIDTH))
    return (b * conv) @ w_out

def padded_len(S, window):
    return -(-S // window) * window

def to_blocks(t, dilation, blk, seq_pad):
    B, S = t.shape[:2]
    t = jnp.pad(t, [(0, 0), (0, seq_pad - S)] + [(0, 0)] * (t.ndim - 2))
    return t.reshape(B, seq_pad // (dilation * blk), blk, dilation, *t.shape[2:])

def kv_context(tb):
    prev = jnp.pad(tb, [(0, 0), (1, 0)] + [(0, 0)] * 4)[:, :-1]
    return jnp.concatenate([prev, tb], axis=2)

def dilated_branch(q, k_ctx, v_ctx, window, dilation, slopes):
    B, S, H, dh = q.shape
    blk = window // dilation
    seq_pad = padded_len(S, window)
    qb = to_blocks(q, dilation, blk, seq_pad)
    nb = qb.shape[1]
    s = jnp.einsum('bnqrhd,bnkrhd->bnrhqk', qb, k_ctx).astype(jnp.float32) * (dh ** -0.5)
    a = jnp.arange(blk)[:, None]
    c = jnp.arange(2 * blk)[None, :]
    j = blk + a - c
    n = jnp.arange(nb)[:, None, None]
    valid = (j >= 0) & (j <= blk) & ((n > 0) | (c >= blk))
    bias = -slopes[:, None, None] * (dilation * j).astype(jnp.float32)
    s = jnp.where(valid[None, :, None, None], s + bias, NEG_INF)
    lse = jax.nn.logsumexp(s, axis=-1)
    p = jnp.exp(s - lse[..., None]).astype(v_ctx.dtype)
    o = jnp.einsum('bnrhqk,bnkrhd->bnqrhd', p, v_ctx).reshape(B, seq_pad, H, dh)[:, :S]
    lse = jnp.transpose(lse, (0, 1, 4, 2, 3)).reshape(B, seq_pad, H)[:, :S]
    return o, lse

def setup_inputs(seed: int = 0) -> dict:
    key = jax.random.key(seed)
    ks = jax.random.split(key, 14)
    n_a = N_A_LAYERS
    n_b = DEPTH - N_A_LAYERS
    qw = N_GROUPS * H_G * HEAD_DIM
    f32 = jnp.float32
    nrm = lambda k, shape: jax.random.normal(k, shape, f32)
    return {
        'x': nrm(ks[0], (BATCH, SEQ, D_MODEL)),
        'norm_mix': 1.0 + 0.05 * nrm(ks[1], (DEPTH, D_MODEL)),
        'norm_mlp': 1.0 + 0.05 * nrm(ks[2], (DEPTH, D_MODEL)),
        'w_a_in': nrm(ks[3], (n_a, D_MODEL, 3 * D_MODEL)) * D_MODEL ** -0.5,
        'conv_w': nrm(ks[4], (n_a, CONV_WIDTH, D_MODEL)) * CONV_WIDTH ** -0.5,
        'w_a_out': nrm(ks[5], (n_a, D_MODEL, D_MODEL)) * D_MODEL ** -0.5,
        'norm_kv': 1.0 + 0.05 * nrm(ks[6], (D_MODEL,)),
        'w_kv': nrm(ks[7], (D_MODEL, 2 * qw)) * D_MODEL ** -0.5,
        'w_q': nrm(ks[8], (n_b, D_MODEL, qw)) * D_MODEL ** -0.5,
        'w_o': nrm(ks[9], (n_b, H_G * HEAD_DIM, D_MODEL)) * (H_G * HEAD_DIM) ** -0.5,
        'w_up': nrm(ks[10], (DEPTH, D_MODEL, D_FF)) * D_MODEL ** -0.5,
        'w_down': nrm(ks[11], (DEPTH, D_FF, D_MODEL)) * (0.5 * D_FF ** -0.5),
        'norm_final': 1.0 + 0.05 * nrm(ks[12], (D_MODEL,)),
    }

def reference(x, norm_mix, norm_mlp, w_a_in, conv_w, w_a_out, norm_kv, w_kv, w_q, w_o, w_up, w_down, norm_final):
    B, S, _ = x.shape
    slopes = 2.0 ** (-ALIBI_MAX_BIAS * jnp.arange(1, H_G + 1, dtype=jnp.float32) / H_G)
    h = x
    shared = []
    for l in range(DEPTH):
        if l < N_A_LAYERS:
            h = h + short_conv_mixer(rmsnorm(h, norm_mix[l]), w_a_in[l], conv_w[l], w_a_out[l])
        else:
            if l == N_A_LAYERS:
                kv = (rmsnorm(h, norm_kv) @ w_kv).reshape(B, S, N_GROUPS, 2, H_G, HEAD_DIM)
                for g, (window, dil) in enumerate(PATTERNS):
                    blk = window // dil
                    sp = padded_len(S, window)
                    shared.append((kv_context(to_blocks(kv[:, :, g, 0], dil, blk, sp)),
                                   kv_context(to_blocks(kv[:, :, g, 1], dil, blk, sp))))
            i = l - N_A_LAYERS
            q = (rmsnorm(h, norm_mix[l]) @ w_q[i]).reshape(B, S, N_GROUPS, H_G, HEAD_DIM)
            outs, lses = [], []
            for g, (window, dil) in enumerate(PATTERNS):
                o_g, lse_g = dilated_branch(q[:, :, g], shared[g][0], shared[g][1], window, dil, slopes)
                outs.append(o_g.astype(jnp.float32))
                lses.append(lse_g)
            wts = jax.nn.softmax(jnp.stack(lses), axis=0)
            o = jnp.sum(wts[..., None] * jnp.stack(outs), axis=0).astype(h.dtype)
            h = h + o.reshape(B, S, H_G * HEAD_DIM) @ w_o[i]
        hn = rmsnorm(h, norm_mlp[l])
        h = h + jnp.square(jax.nn.relu(hn @ w_up[l])) @ w_down[l]
    return rmsnorm(h, norm_final)


_drawn_inputs = setup_inputs


def setup_inputs(seed=0):
    import zlib

    import numpy as np

    out = dict(_drawn_inputs(seed))
    spreads = {}
    factors = {'norm_kv': 4.213}
    for name, (base, spread) in spreads.items():
        noise = np.random.default_rng([zlib.crc32(name.encode()), seed]).standard_normal(out[name].shape)
        drawn = base * np.exp(spread * noise) if base else spread * noise
        out[name] = __import__('jax').numpy.asarray(drawn.astype(out[name].dtype))
    for name, factor in factors.items():
        out[name] = (out[name] * factor).astype(out[name].dtype)
    return out
```

```python
from contextlib import ExitStack

import concourse.bass as bass
from concourse import mybir

F32 = mybir.dt.float32
F32R = mybir.dt.float32r
ALU = mybir.AluOpType
ACT = mybir.ActivationFunctionType
AX = mybir.AxisListType

P = 128
SEQ = 512
D = 1024
KC = D // P
FF = 4 * D
HALF = FF // 2
ZC = HALF // P
N_GROUPS, H_G, HEAD = 3, 8, 64
PAIRS = H_G // 2
DILATIONS = (1, 4, 16)
TILES = SEQ // P
EPS = 1e-5
MASKED = 2.0 ** 126

PANEL = KC * P
RING = 4
RING_ATT = 3
AHEAD = 2
CREDIT = RING
PER_PAIR = 3 * N_GROUPS

IN0 = 0
OUT0 = IN0 + 3 * KC
MLP0 = OUT0 + KC
HALF_PANELS = ZC + 2 * KC
ATT0 = MLP0 + 2 * HALF_PANELS
WO0 = ATT0 + PAIRS * PER_PAIR
MLP1 = WO0 + KC // 2
N_PANELS = MLP1 + 2 * HALF_PANELS
assert IN0 % RING == OUT0 % RING == MLP0 % RING == ATT0 % RING == WO0 % RING == MLP1 % RING == 0

MIX0, GMLP0, GKV, MIX1, GMLP1, GFIN = (n * KC for n in range(6))
TAPS = 6 * KC
SLOPES = TAPS + 3 * KC
EPSC = SLOPES + H_G
N_CONST = EPSC + 1

SC0, SC1, SC2 = 0, 7 * P, 11 * P
SCORES = 15 * P
SC = (SC0, SC1, SC2)
TILE_COLS = (
    ((0, P), (P, 3 * P), (3 * P, 5 * P), (5 * P, 7 * P)),
    tuple((SC1 + t * P, SC1 + (t + 1) * P) for t in range(TILES)),
    tuple((SC2 + t * P, SC2 + (t + 1) * P) for t in range(TILES)),
)
PIECES = (
    tuple((e, c, tiles) for e in range(2)
          for c, tiles in ((0, ((0, 0, 1), (1, 0, 2))), (3 * P, ((2, 1, 2), (3, 2, 2))))),
    tuple((e, SC1, tuple((t, t, 1) for t in range(TILES))) for e in range(2)),
    tuple((e, SC2, tuple((t, t, 1) for t in range(TILES))) for e in range(2)),
)
PIECE0 = (0, 4, 6)
LOTS = (
    (((0, 0, 4), (1, 4, 3)), ((2, 0, 4), (3, 4, 3))),
    (((4, 0, 4),), ((5, 0, 4),)),
    (((6, 0, 4),), ((7, 0, 4),)),
)
ATTEND_AT, SCORES_AT, TURN_AT = (1, 2, 4), (2, 4, 6), (7, 8)
MAXES = N_GROUPS * TILES * 2


class Steps:

    def __init__(self):
        self.before, self.here, self.turn, self.per = 0, 0, 0, 0

    def add(self):
        self.here += 1
        return 1

    def count(self):
        return self.turn * self.per + (self.before + self.here) if self.per else self.before + self.here

    def enter(self, turn, per):
        self.before, self.here, self.turn, self.per = self.before + self.here, 0, turn, per

    def leave(self, turns):
        assert self.here == self.per, (self.here, self.per)
        self.before, self.here, self.turn, self.per = self.before + turns * self.per, 0, 0, 0


def yoco_trunk(nc, x_t, weights, consts, dist, ident, out_t, scratch):
    ctx = ExitStack()
    with ctx:
        base = (nc.sbuf_base + 63) // 64 * 64
        slab = ctx.enter_context(nc.sbuf_tensor("slab", [P, (nc.sbuf_usable_end - base - 128) // 4], F32))
        at = [base]
        end = nc.sbuf_usable_end - 64

        def place(name, shape, dt, offset=None):
            size = 4
            for n in shape:
                size *= n
            where = at[0] if offset is None else offset
            if offset is None:
                at[0] += (size + 31) // 32 * 32
                assert at[0] <= end, (name, at[0] - end)
            t = nc.alloc_sbuf_tensor_at(name, [P, *shape], dtype=dt, offset=where)
            return t, where + (size + 31) // 32 * 32

        h, _ = place("h", [KC, SEQ], F32)
        xn_hi, _ = place("xn_hi", [KC, SEQ], F32R)
        xn_lo, _ = place("xn_lo", [KC, SEQ], F32R)
        kv_area = at[0]
        xkv_hi, _ = place("xkv_hi", [KC, SEQ], F32R)
        xkv_lo, _ = place("xkv_lo", [KC, SEQ], F32R)
        z_area = at[0]
        z_hi, _ = place("z_hi", [ZC, SEQ], F32R)
        z_lo, z_end = place("z_lo", [ZC, SEQ], F32R)
        w_raw, _ = place("w_raw", [RING, PANEL], F32)
        w_hi, _ = place("w_hi", [RING, PANEL], F32R)
        w_lo, _ = place("w_lo", [RING, PANEL], F32R)
        rstd, _ = place("rstd", [SEQ], F32)
        rstd2, _ = place("rstd2", [SEQ], F32)
        sq_sum, _ = place("sq_sum", [SEQ], F32)
        sq, _ = place("sq", [SEQ], F32)
        tmp, _ = place("tmp", [2, SEQ], F32)
        tmp2, _ = place("tmp2", [SEQ], F32)
        cst, _ = place("cst", [N_CONST], F32)
        ones, _ = place("ones", [P], F32)
        idn, _ = place("idn", [P], F32)
        cu, nxt = place("cu", [SEQ + 2], F32, kv_area)
        conv, nxt = place("conv", [3, SEQ], F32, nxt)
        gate, nxt = place("gate", [SEQ], F32, nxt)
        mixed, nxt = place("mixed", [SEQ], F32, nxt)
        final, _ = place("final", [KC, SEQ], F32, kv_area)
        o_hi, nxt = place("o_hi", [PAIRS, SEQ], F32R, kv_area)
        o_lo, _ = place("o_lo", [PAIRS, SEQ], F32R, nxt)
        k_t, nxt = place("k_t", [N_GROUPS, SEQ], F32, z_area)
        q_t, nxt = place("q_t", [N_GROUPS, SEQ], F32, nxt)
        sc, nxt = place("sc", [2, SCORES], F32, nxt)
        p_t, nxt = place("p_t", [4, SEQ], F32, nxt)
        v_sb, nxt = place("v_sb", [N_GROUPS, TILES, 3 * HEAD], F32, nxt)
        v_t, nxt = place("v_t", [2, SEQ], F32, nxt)
        dst, nxt = place("dst", [7 * P], F32, nxt)
        rec, nxt = place("rec", [SEQ], F32, nxt)
        o_t, nxt = place("o_t", [PAIRS, SEQ], F32, nxt)
        mx, nxt = place("mx", [MAXES], F32, nxt)
        mall, nxt = place("mall", [N_GROUPS, N_GROUPS, TILES * 2], F32, nxt)
        negm, nxt = place("negm", [MAXES], F32, nxt)
        joint, nxt = place("joint", [MAXES], F32, nxt)
        slope_now, nxt = place("slope_now", [2], F32, nxt)
        assert nxt <= z_end, nxt - z_end
        acc = tmp

        banks = [ctx.enter_context(nc.psum_tensor(f"bank{n}", [P, SEQ], F32)) for n in range(8)]
        STAT = O_BANK = 7
        S_BANK, T_BANK = 3, 5

        def sem(name):
            return ctx.enter_context(nc.semaphore(name))

        raw_ready = [sem(f"raw_ready{n}") for n in range(RING)]
        x_ready = [sem(f"x_ready{n}") for n in range(KC)]
        cst_ready, idn_ready, dst_ready = sem("cst_ready"), sem("idn_ready"), sem("dst_ready")
        ones_ready = sem("ones_ready")
        vones_ready = sem("vones_ready")
        hi_done = sem("hi_done")
        lo_done = sem("lo_done")
        panel_done = sem("panel_done")
        bank_free = sem("bank_free")
        xhi_done = sem("xhi_done")
        kvhi_done = sem("kvhi_done")
        zhi_done = sem("zhi_done")
        ohi_done = sem("ohi_done")
        xn_ready, xkv_ready = sem("xn_ready"), sem("xkv_ready")
        z_ready, o_ready = sem("z_ready"), sem("o_ready")
        r_done = sem("r_done")
        mixed_ready = sem("mixed_ready")
        h_ready = sem("h_ready")
        sq_step = sem("sq_step")
        sq_ready = sem("sq_ready")
        ss_done = sem("ss_done")
        std_done = sem("std_done")
        rstd_ready = sem("rstd_ready")
        dve_step = sem("dve_step")
        s_done, s_used = sem("s_done"), sem("s_used")
        mx_ready = sem("mx_ready")
        mx_out, mx_in = sem("mx_out"), sem("mx_in")
        negm_ready = sem("negm_ready")
        p_ready = sem("p_ready")
        t_done, t_used = sem("t_done"), sem("t_used")
        ob_filled, ob_free = sem("ob_filled"), sem("ob_free")
        ot_ready = sem("ot_ready")
        out_ready, out_done = sem("out_ready"), sem("out_done")

        X_IN, X_MLP0, X_MIX1, X_MLP1 = 0, KC, 2 * KC, 3 * KC
        Z_Y, Z_MLP0, Z_MLP1 = 0, KC, KC + 2 * ZC

        def order(ap, group):
            r = DILATIONS[group]
            return ap if r == 1 else ap.rearrange("p (i r) -> p r i", r=r)

        def grouped(ap, group):
            r = DILATIONS[group]
            return ap if r == 1 else ap.rearrange("p (r i) -> p r i", r=r)

        def landed(phase, slot):
            fills = min(phase, ATT0) // RING
            if phase > ATT0:
                fills += (PAIRS * PER_PAIR // RING_ATT if slot < RING_ATT else 0) + (phase - WO0) // RING
            return fills

        block = ctx.enter_context(nc.Block())

        @block.sync
        def _(sp):
            def load(p, slot, ring=RING):
                sp.wait_ge(lo_done, p + (1 - ring + CREDIT))
                sp.dma_start(w_raw[:, slot, :], weights[p]).then_inc(raw_ready[slot], 16)

            sp.dma_start(cst[:, :], consts).then_inc(cst_ready, 16)
            load(0, 0)
            for k in range(KC):
                sp.dma_start(h[:, k, :], x_t[k]).then_inc(x_ready[k], 16)
            for p in range(1, RING):
                load(p, p)
            sp.dma_start(idn[:, :], ident).then_inc(idn_ready, 16)
            with sp.Fori(1, ATT0 // RING) as i:
                for c in range(RING):
                    load(i * RING + c, c)
            for q in range(RING_ATT):
                load(ATT0 + q, q, RING_ATT)
            sp.wait_ge(panel_done, ATT0 + CREDIT)
            sp.dma_start(dst[:, :], dist).then_inc(dst_ready, 16)
            strided = scratch.rearrange("g (i c r) e -> g r i c e", c=TILES, r=4)
            with sp.Fori(0, PAIRS) as i:
                for q in range(PER_PAIR):
                    load(i * PER_PAIR + (ATT0 + RING_ATT + q), q % RING_ATT, RING_ATT)
                sp.wait_ge(mx_ready, i + 1)
                m = mx[:, :].rearrange("p (g t e) -> p g t e", g=N_GROUPS, e=2)
                sp.dma_start(scratch[0].rearrange("(t p) e -> p t e", p=P), m[:, 0]).then_inc(mx_out, 16)
                sp.dma_start(scratch[1].rearrange("(p t) e -> p t e", p=P), m[:, 1]).then_inc(mx_out, 16)
                for r in range(4):
                    sp.dma_start(strided[2, r], m[32 * r:32 * r + 32, 2]).then_inc(mx_out, 16)
                sp.wait_ge(mx_out, i * 96 + 96)
                a = mall[:, :, :, :].rearrange("p g a (t e) -> p g a t e", e=2)
                for s in range(N_GROUPS):
                    sp.dma_start(a[:, 0, s], scratch[s].rearrange("(t p) e -> p t e", p=P)).then_inc(mx_in, 16)
                    sp.dma_start(a[:, 1, s], scratch[s].rearrange("(p t) e -> p t e", p=P)).then_inc(mx_in, 16)
                    for r in range(4):
                        sp.dma_start(a[32 * r:32 * r + 32, 2, s], strided[s, r]).then_inc(mx_in, 16)
            load(MLP1 - 1, RING - 1)
            with sp.Fori(MLP1 // RING, N_PANELS // RING) as i:
                for c in range(RING):
                    load(i * RING + c, c)
            for k in range(KC):
                sp.wait_ge(out_ready, k + 1)
                sp.dma_start(out_t[k], final[:, k, :]).then_inc(out_done, 16)
            sp.wait_ge(out_done, 16 * KC)

        @block.tensor
        def _(pe):
            pe.sem_inc(panel_done, CREDIT)

            def products(out, slot, col, hi, lo, chunks, first, last, ready=None):
                for n, k in enumerate(chunks):
                    if ready is not None:
                        pe.wait_ge(ready[0], ready[1] + k + 1)
                    w = slice(col + n * P, col + (n + 1) * P)
                    pe.matmul(out, w_hi[:, slot, w], hi[:, k, :], start=first and n == 0, stop=False)
                    pe.matmul(out, w_hi[:, slot, w], lo[:, k, :], start=False, stop=False)
                    mm = pe.matmul(out, w_lo[:, slot, w], hi[:, k, :], start=False,
                                   stop=last and n == len(chunks) - 1)
                return mm

            def panel(p, slot, bank, hi, lo, chunks=range(KC), first=True, last=True, ready=None):
                pe.wait_ge(lo_done, p + (1 + CREDIT))
                if first:
                    pe.wait_ge(bank_free, p + (1 - RING + CREDIT))
                products(banks[bank][:, :], slot, 0, hi, lo, chunks, first, last, ready).then_inc(panel_done, 1)

            def stats(n):
                pe.wait_ge(sq_ready, n + 1)
                pe.matmul(banks[STAT][:, :], ones[:, :], sq_sum[:, :], start=True, stop=True).then_inc(ss_done, 1)

            def mlp(p0, x_count, z_count, norm):
                for half in range(2):
                    up, down = p0 + half * HALF_PANELS, p0 + half * HALF_PANELS + ZC
                    with pe.Fori(0, ZC // RING) as i:
                        for c in range(RING):
                            panel(i * RING + (up + c), c, c, xn_hi, xn_lo,
                                  ready=(xn_ready, x_count) if c == 0 else None)
                    if half == 0:
                        stats(norm)
                    with pe.Fori(0, 2 * KC // 8) as i:
                        for c in range(8):
                            k0 = KC * (c % 2)
                            panel(i * 8 + (down + c), c % RING, c // 2, z_hi, z_lo, chunks=range(k0, k0 + KC),
                                  first=c % 2 == 0, last=c % 2 == 1,
                                  ready=(z_ready, z_count + half * ZC) if c < 2 else None)

            pe.wait_ge(ones_ready, 1)
            for c in range(RING):
                panel(IN0 + c, c, c, xn_hi, xn_lo, ready=(xn_ready, X_IN) if c == 0 else None)
                if c == 1:
                    stats(0)
            with pe.Fori(1, 3 * KC // RING) as i:
                for c in range(RING):
                    panel(i * RING + (IN0 + c), c, c, xn_hi, xn_lo)
            with pe.Fori(0, KC // RING) as i:
                for c in range(RING):
                    panel(i * RING + (OUT0 + c), c, c, z_hi, z_lo, ready=(z_ready, Z_Y) if c == 0 else None)
            mlp(MLP0, X_MLP0, Z_MLP0, 1)

            def scores(i, g):
                pe.wait_ge(bank_free, i * PER_PAIR + (ATT0 + 2 * g + 2 + CREDIT))
                for n, (e, _, tiles) in enumerate(PIECES[g]):
                    n += PIECE0[g]
                    pe.wait_ge(s_used, i * 8 + (n + 1))
                    rows = slice(HEAD * e, HEAD * e + HEAD)
                    bank, col = banks[S_BANK + n % 2], 0
                    for tile, key, nk in tiles:
                        mm = pe.matmul(bank[:, col:col + nk * P], q_t[rows, g, tile * P:(tile + 1) * P],
                                       k_t[rows, g, key * P:(key + nk) * P], start=True, stop=True)
                        col += nk * P
                    mm.then_inc(s_done, 1)

            def turn_v(i, g):
                pe.wait_ge(bank_free, i * PER_PAIR + (ATT0 + 6 + g + 1 + CREDIT))
                pe.wait_ge(ob_free, i * 9 + (g + 1))
                for t in range(TILES):
                    mm = pe.transpose(banks[O_BANK][:, t * P:(t + 1) * P], v_t[:, g % 2, t * P:(t + 1) * P],
                                      idn[:, :])
                mm.then_inc(ob_filled, 1)

            def attend(i, g):
                pe.wait_ge(p_ready, i * 3 + (g + 1))
                for e in range(2):
                    for n, tile, nt in LOTS[g][e]:
                        pe.wait_ge(t_used, i * 8 + (n + 1))
                        for t in range(nt):
                            c = SC[g] + (tile + t) * P
                            mm = pe.transpose(banks[T_BANK + n % 2][:, t * P:(t + 1) * P], sc[:, e, c:c + P],
                                              idn[:, :])
                        mm.then_inc(t_done, 1)
                out = banks[O_BANK]
                for e in range(2):
                    vcols = slice(HEAD * e, HEAD * e + P)
                    pe.wait_ge(ob_free, i * 9 + (4 + 2 * g + e))
                    for n, tile, nt in LOTS[g][e]:
                        pe.wait_ge(t_used, i * 8 + (n + 3))
                        if g == 0:
                            for key in (tile // 2, tile // 2 + 1):
                                nq = min(2, TILES - key)
                                c = (2 * key - tile) * P
                                mm = pe.matmul(out[:, key * P:(key + nq) * P], v_sb[:, g, key, vcols],
                                               p_t[:, n % 4, c:c + nq * P], start=key == 0,
                                               stop=key == TILES - 1, skip_group_check=True)
                        else:
                            for t in range(TILES):
                                mm = pe.matmul(out[:, t * P:(t + 1) * P], v_sb[:, g, t, vcols],
                                               p_t[:, n % 4, t * P:(t + 1) * P], start=True, stop=True)
                    mm.then_inc(ob_filled, 1)

            def pair(i, first):
                for q in range(PER_PAIR):
                    hi, lo = (xn_hi, xn_lo) if q in (1, 3, 5) else (xkv_hi, xkv_lo)
                    ready = ((xkv_ready, 0), (xn_ready, X_MIX1))[q] if first and q < 2 else None
                    panel(i * PER_PAIR + (ATT0 + q), q % RING_ATT, q % RING_ATT, hi, lo, ready=ready)
                    if first and q == 0:
                        stats(2)
                    if not first and q == 0:
                        turn_v(i - 1, 2)
                    if not first and q in ATTEND_AT:
                        attend(i - 1, ATTEND_AT.index(q))
                    if q in SCORES_AT:
                        scores(i, SCORES_AT.index(q))
                    if q in TURN_AT:
                        turn_v(i, q - TURN_AT[0])

            pe.wait_ge(idn_ready, 16)
            pair(0, True)
            pe.wait_ge(vones_ready, 1)
            with pe.Fori(1, PAIRS) as i:
                pair(i, False)

            turn_v(PAIRS - 1, 2)
            pe.wait_ge(bank_free, WO0 + CREDIT)
            pe.wait_ge(s_used, 8 * PAIRS + 2)
            pe.wait_ge(o_ready, 1)
            for c in range(2):
                pe.wait_ge(lo_done, WO0 + c + 1 + CREDIT)
                for s in range(2):
                    products(banks[2 * c + s][:, :], c, s * PAIRS * P, o_hi, o_lo, range(PAIRS - 1), True, False)
            for g in range(N_GROUPS):
                attend(PAIRS - 1, g)
            pe.wait_ge(o_ready, 2)
            for c in range(4):
                pe.wait_ge(lo_done, WO0 + c + 1 + CREDIT)
                for s in range(2):
                    done = PAIRS - 1 if c < 2 else 0
                    mm = products(banks[2 * c + s][:, :], c, (s * PAIRS + done) * P, o_hi, o_lo,
                                  range(done, PAIRS), done == 0, True)
                mm.then_inc(panel_done, 1)
            mlp(MLP1, X_MLP1, Z_MLP1, 3)
            stats(4)

        @block.scalar
        def _(act):
            act.sem_inc(t_used, 2)

            def split(p, slot, fills, ring=RING):
                act.wait_ge(raw_ready[slot], fills * 16)
                act.wait_ge(panel_done, p + (1 - ring + CREDIT))
                act.copy(w_hi[:, slot, :], w_raw[:, slot, :]).then_inc(hi_done, 1)

            def ahead(phase, turn, c, rings=1):
                slot = (c + AHEAD) % RING
                split(turn * (rings * RING) + (phase + c + AHEAD), slot,
                      turn * rings + (landed(phase, slot) + 1 + (c + AHEAD) // RING))

            def normed(hi, gain, j, done):
                act.activation(hi[:, j, :], h[:, j, :], ACT.Copy, scale=cst[:, bass.ds(j + gain, 1)]).then_inc(done, 1)

            def root(n):
                act.wait_ge(ss_done, n + 1)
                act.activation(rstd2[:, :], banks[STAT][:, :], ACT.Sqrt, scale=1.0 / D,
                               bias=cst[:, EPSC:EPSC + 1]).then_inc(std_done, 1)

            def mlp(p0, z_count, norm, h_count, gains):
                for half in range(2):
                    up, down = p0 + half * HALF_PANELS, p0 + half * HALF_PANELS + ZC
                    relus = half * ZC + (0 if p0 == MLP0 else 2 * ZC)
                    with act.Fori(0, ZC // RING) as i:
                        for c in range(RING):
                            p = i * RING + (up + c)
                            ahead(up, i, c)
                            act.wait_ge(bank_free, p + (1 - 2 + CREDIT))
                            act.wait_ge(panel_done, p + (1 + CREDIT))
                            act.activation(tmp[:, c % 2, :], banks[c][:, :], ACT.Relu).then_inc(r_done, 1)
                            act.wait_ge(r_done, i * RING + (relus + c + 1))
                            act.activation(z_hi[:, i * RING + c, :], tmp[:, c % 2, :], ACT.Square).then_inc(zhi_done, 1)
                    if half == 0:
                        root(norm)

                    def down_turn(i):
                        for c in range(2 * RING):
                            if not (isinstance(i, int) and down + i * 2 * RING + c + AHEAD >= N_PANELS):
                                ahead(down, i, c, 2)
                            if half == 1 and c % 2 == 1 and gains:
                                act.wait_ge(h_ready, i * RING + (h_count + c // 2 + 1))
                                for hi, gain, done in gains:
                                    normed(hi, gain, i * RING + c // 2, done)
                    if half == 1 and p0 == MLP1:
                        for i in range(2):
                            down_turn(i)
                    else:
                        with act.Fori(0, 2) as i:
                            down_turn(i)

            act.wait_ge(cst_ready, 16)
            split(0, 0, 1)
            for k in range(KC):
                act.wait_ge(x_ready[k], 16)
                normed(xn_hi, MIX0, k, xhi_done)
            split(1, 1, 1)
            root(0)
            with act.Fori(0, KC // RING) as i:
                for c in range(3 * RING):
                    ahead(IN0, i, c, 3)
                    if c % 3 == 2:
                        act.wait_ge(mixed_ready, i * RING + (c // 3 + 1))
                        act.copy(z_hi[:, i * RING + c // 3, :], mixed[:, :]).then_inc(zhi_done, 1)
            with act.Fori(0, KC // RING) as i:
                for c in range(RING):
                    ahead(OUT0, i, c)
                    act.wait_ge(bank_free, i * RING + (OUT0 + c + 1 + CREDIT))
                    normed(xn_hi, GMLP0, i * RING + c, xhi_done)
            mlp(MLP0, Z_MLP0, 1, 0, ((xn_hi, MIX1, xhi_done), (xkv_hi, GKV, kvhi_done)))

            def exps(i, g):
                act.wait_ge(negm_ready, i + 1)
                for e in range(2):
                    for t in range(TILES):
                        cols = slice(*TILE_COLS[g][t])
                        m = (g * TILES + t) * 2 + e
                        ins = act.activation(sc[:, e, cols], sc[:, e, cols], ACT.Exp, bias=negm[:, m:m + 1])
                ins.then_inc(p_ready, 1)

            def copy_pt(i, g):
                for e in range(2):
                    for n, _, nt in LOTS[g][e]:
                        act.wait_ge(t_done, i * 8 + (n + 1))
                        act.wait_ge(ob_filled, i * 9 + (3 if n < 4 else 4 + (n - 4) // 2))
                        act.copy(p_t[:, n % 4, 0:nt * P], banks[T_BANK + n % 2][:, 0:nt * P]).then_inc(t_used, 1)

            def pair(i, first):
                for q in range(PER_PAIR):
                    a = q + AHEAD
                    slot = a % RING_ATT
                    split(i * PER_PAIR + (ATT0 + a), slot,
                          i * (PER_PAIR // RING_ATT) + (landed(ATT0, slot) + a // RING_ATT + 1), RING_ATT)
                    if not first and q < N_GROUPS:
                        exps(i - 1, q)
                    if not first and q in ATTEND_AT:
                        copy_pt(i - 1, ATTEND_AT.index(q))

            root(2)
            pair(0, True)
            with act.Fori(1, PAIRS) as i:
                pair(i, False)
            for c in range(2):
                a = c + AHEAD
                split(WO0 + a, a, landed(WO0, a) + 1, RING_ATT if c == 0 else RING)
            act.wait_ge(panel_done, WO0 + CREDIT)
            act.wait_ge(ot_ready, PAIRS - 1)
            act.copy(o_hi[:, 0:PAIRS - 1, :], o_t[:, 0:PAIRS - 1, :]).then_inc(ohi_done, 1)
            for g in range(N_GROUPS):
                exps(PAIRS - 1, g)
            for g in range(N_GROUPS):
                copy_pt(PAIRS - 1, g)
            act.wait_ge(ot_ready, PAIRS)
            act.copy(o_hi[:, PAIRS - 1, :], o_t[:, PAIRS - 1, :]).then_inc(ohi_done, 1)
            for c in range(RING):
                if c >= 2:
                    ahead(WO0, 0, c)
                for s in range(2):
                    act.wait_ge(h_ready, KC + 2 * c + s + 1)
                    normed(xn_hi, GMLP1, 2 * c + s, xhi_done)
            mlp(MLP1, Z_MLP1, 3, 2 * KC, ())
            root(4)

        @block.vector
        def _(dve):
            dve.sem_inc(lo_done, CREDIT)
            dve.sem_inc(bank_free, CREDIT)
            dve.sem_inc(s_used, 2)
            dve.sem_inc(ob_free, 1)
            steps = Steps()

            def lo_part(lo, x, hi, done):
                dve.tensor_tensor(lo, x, hi.bitcast(F32), ALU.subtract).then_inc(done, 1)

            def split(p, slot):
                dve.wait_ge(hi_done, p + 1)
                lo_part(w_lo[:, slot, :], w_raw[:, slot, :], w_hi[:, slot, :], lo_done)

            def ahead(phase, turn, c, rings=1):
                split(turn * (rings * RING) + (phase + c + AHEAD), (c + AHEAD) % RING)

            def normed(hi, lo, gain, j, counted, count, done):
                dve.wait_ge(counted, count)
                dve.scalar_tensor_tensor(out=lo[:, j, :], in0=h[:, j, :], scalar=cst[:, bass.ds(j + gain, 1)],
                                         in1=hi[:, j, :].bitcast(F32), op0=ALU.mult,
                                         op1=ALU.subtract).then_inc(done, 1)

            def inverse_rms(n):
                dve.wait_ge(std_done, n + 1)
                dve.tensor_scalar(tmp2[:, :], banks[STAT][:, :], 1.0 / D, EPS, ALU.mult,
                                  ALU.add).then_inc(dve_step, steps.add())
                dve.reciprocal(rstd[:, :], rstd2[:, :]).then_inc(dve_step, steps.add())
                for _ in range(2):
                    dve.wait_ge(dve_step, steps.count())
                    dve.tensor_tensor(tmp2[:, :], tmp2[:, :], rstd[:, :], ALU.mult).then_inc(dve_step, steps.add())
                dve.wait_ge(dve_step, steps.count())
                dve.tensor_scalar(tmp2[:, :], tmp2[:, :], -0.5, 1.5, ALU.mult, ALU.add).then_inc(dve_step, steps.add())
                dve.wait_ge(dve_step, steps.count())
                dve.tensor_tensor(rstd[:, :], rstd[:, :], tmp2[:, :], ALU.mult).then_inc(dve_step, steps.add())
                dve.wait_ge(dve_step, steps.count())
                dve.tensor_tensor(rstd2[:, :], rstd[:, :], rstd[:, :], ALU.mult).then_inc(dve_step, steps.add())
                dve.wait_ge(dve_step, steps.count())

            def mlp(p0, z_count, norm, gains):
                for half in range(2):
                    up, down = p0 + half * HALF_PANELS, p0 + half * HALF_PANELS + ZC
                    relus = half * ZC + (0 if p0 == MLP0 else 2 * ZC)
                    with dve.Fori(0, ZC // RING) as i:
                        for c in range(RING):
                            ahead(up, i, c)
                            dve.wait_ge(z_ready, i * RING + (z_count + half * ZC + c))
                            dve.wait_ge(r_done, i * RING + (relus + c + 1))
                            dve.tensor_tensor(tmp2[:, :], tmp[:, c % 2, :], tmp[:, c % 2, :],
                                              ALU.mult).then_inc(bank_free, 1)
                            dve.wait_ge(bank_free, i * RING + (up + c + 1 + CREDIT))
                            dve.wait_ge(zhi_done, i * RING + (z_count + half * ZC + c + 1))
                            lo_part(z_lo[:, i * RING + c, :], tmp2[:, :], z_hi[:, i * RING + c, :], z_ready)
                    dve.wait_ge(z_ready, z_count + (half + 1) * ZC)
                    if half == 0:
                        inverse_rms(norm)

                    def down_turn(i):
                        for c in range(2 * RING):
                            if not (isinstance(i, int) and down + i * 2 * RING + c + AHEAD >= N_PANELS):
                                ahead(down, i, c, 2)
                            if c % 2 == 0:
                                continue
                            dve.wait_ge(dve_step, steps.count())
                            j, p = i * RING + c // 2, i * 2 * RING + (down + c)
                            dve.wait_ge(panel_done, p + (1 + CREDIT))
                            dve.tensor_tensor(tmp2[:, :], banks[c // 2][:, :], rstd2[:, :], ALU.mult).then_inc(bank_free, 2)
                            dve.wait_ge(bank_free, p + (1 + CREDIT))
                            if half == 0:
                                dve.tensor_tensor(h[:, j, :], h[:, j, :], tmp2[:, :],
                                                  ALU.add).then_inc(dve_step, steps.add())
                                continue
                            dve.tensor_tensor(h[:, j, :], h[:, j, :], tmp2[:, :], ALU.add).then_inc(h_ready, 1)
                            dve.wait_ge(h_ready, j + ((0 if p0 == MLP0 else 2 * KC) + 1))
                            for hi, lo, gain, counted, count, done in gains:
                                normed(hi, lo, gain, j, counted, j + (count + 1), done)
                    if half == 1 and p0 == MLP1:
                        for i in range(2):
                            down_turn(i)
                    else:
                        with dve.Fori(0, 2) as i:
                            steps.enter(i, RING * (1 - half))
                            down_turn(i)
                            steps.leave(2)
                    dve.wait_ge(dve_step, steps.count())

            dve.wait_ge(cst_ready, 16)
            split(0, 0)
            for k in range(KC):
                normed(xn_hi, xn_lo, MIX0, k, xhi_done, X_IN + k + 1, xn_ready)
            split(1, 1)
            inverse_rms(0)
            dve.wait_ge(ones_ready, 2)

            with dve.Fori(0, KC // RING) as i:
                steps.enter(i, 3 * RING)
                for n in range(RING):
                    j = i * RING + n
                    tap = [cst[:, bass.ds(j + (TAPS + k * KC), 1)] for k in range(3)]
                    for part in range(3):
                        c = 3 * n + part
                        p = i * 3 * RING + (IN0 + c)
                        ahead(IN0, i, c, 3)
                        dve.wait_ge(panel_done, p + (1 + CREDIT))
                        bank = banks[c % RING][:, :]
                        if part == 0:
                            dve.tensor_tensor(gate[:, :], bank, rstd2[:, :], ALU.mult).then_inc(bank_free, 1)
                            dve.wait_ge(bank_free, p + (1 + CREDIT))
                        elif part == 1:
                            dve.tensor_tensor(cu[:, 2:], gate[:, :], bank, ALU.mult).then_inc(bank_free, 1)
                            dve.wait_ge(bank_free, p + (1 + CREDIT))
                            dve.tensor_scalar(conv[:, 0, :], cu[:, 2:], tap[0], None,
                                              ALU.mult).then_inc(dve_step, steps.add())
                            for k in (1, 2):
                                dve.wait_ge(dve_step, steps.count())
                                dve.scalar_tensor_tensor(out=conv[:, k, :], in0=cu[:, 2 - k:2 - k + SEQ],
                                                         scalar=tap[k], in1=conv[:, k - 1, :], op0=ALU.mult,
                                                         op1=ALU.add).then_inc(dve_step, steps.add())
                        else:
                            dve.tensor_tensor(gate[:, :], bank, rstd[:, :], ALU.mult).then_inc(bank_free, 1)
                            dve.wait_ge(bank_free, p + (1 + CREDIT))
                            dve.wait_ge(dve_step, steps.count())
                            dve.tensor_tensor(mixed[:, :], conv[:, 2, :], gate[:, :], ALU.mult).then_inc(mixed_ready, 1)
                            dve.wait_ge(zhi_done, j + 1)
                            lo_part(z_lo[:, j, :], mixed[:, :], z_hi[:, j, :], z_ready)
                steps.leave(KC // RING)
            with dve.Fori(0, KC // RING) as i:
                for c in range(RING):
                    j = i * RING + c
                    ahead(OUT0, i, c)
                    dve.wait_ge(panel_done, j + (OUT0 + 1 + CREDIT))
                    dve.tensor_tensor(h[:, j, :], h[:, j, :], banks[c][:, :], ALU.add).then_inc(bank_free, 1)
                    normed(xn_hi, xn_lo, GMLP0, j, xhi_done, j + (X_MLP0 + 1), xn_ready)
            mlp(MLP0, Z_MLP0, 1, ((xn_hi, xn_lo, MIX1, xhi_done, X_MIX1, xn_ready),
                                  (xkv_hi, xkv_lo, GKV, kvhi_done, 0, xkv_ready)))

            def copy_v(i, g):
                dve.wait_ge(ob_filled, i * 9 + (g + 1))
                v = v_sb[:, g, :, :].rearrange("p t (a c) -> p t a c", c=HEAD)[:, :, 0:3:2, :]
                dve.tensor_copy(v, banks[O_BANK][:, :].rearrange("p (t a c) -> p t a c", t=TILES,
                                                                 a=2)).then_inc(ob_free, 1)

            def combine(i, g):
                for e in range(2):
                    unit = 2 * g + e
                    dve.wait_ge(ob_filled, i * 9 + (4 + unit))
                    if g == 0:
                        dve.tensor_copy(acc[:, e, :], banks[O_BANK][:, :]).then_inc(ob_free, 1)
                    else:
                        dve.wait_ge(ob_free, i * 9 + (3 + unit))
                        total = order(acc[:, e, :], g)
                        dve.tensor_tensor(total, total, grouped(banks[O_BANK][:, :], g), ALU.add).then_inc(ob_free, 1)

            def normalize(i):
                dve.wait_ge(ob_free, i * 9 + 10)
                low, high = slice(0, HEAD), slice(HEAD, P)
                dve.reciprocal(rec[low, :], acc[high, 0, :]).then_inc(dve_step, steps.add())
                dve.reciprocal(rec[high, :], acc[low, 1, :]).then_inc(dve_step, steps.add())
                dve.wait_ge(dve_step, steps.count())
                dve.tensor_tensor(o_t[low, i, :], acc[low, 0, :], rec[low, :], ALU.mult).then_inc(dve_step, steps.add())
                dve.tensor_tensor(o_t[high, i, :], acc[high, 1, :], rec[high, :], ALU.mult).then_inc(ot_ready, 1)

            def score_pieces(i, g):
                def maxima(n, e, c0, tiles):
                    dve.wait_ge(s_used, i * 8 + (n + 3))
                    if g == 0 and n % 2 == 0:
                        runs = [(0, 1, 1), (1, 1, 2)]
                    else:
                        runs = [(tiles[0][0], len(tiles), tiles[0][2])]
                    for t, nt, nk in runs:
                        m0 = (g * TILES + t) * 2 + e
                        s = sc[:, e, c0:c0 + nt * nk * P].rearrange("p (t k) -> p t k", t=nt)
                        ins = dve.tensor_reduce(mx[:, m0:m0 + 2 * (nt - 1) + 1:2], s, AX.X, ALU.max)
                        c0 += nt * nk * P
                    return ins
                before = None
                for n, (e, c0, tiles) in enumerate(PIECES[g]):
                    n += PIECE0[g]
                    width = sum(nk for _, _, nk in tiles) * P
                    dve.wait_ge(s_done, i * 8 + (n + 1))
                    bank = banks[S_BANK + n % 2][:, 0:width]
                    out = sc[:, e, c0:c0 + width]
                    if g == 0:
                        far = dst[:, (0 if n % 2 == 0 else P):][:, 0:width]
                    else:
                        far = dst[:, (4 + g) * P:(5 + g) * P].unsqueeze(1).broadcast_to([P, TILES, P])
                        bank, out = (a.rearrange("p (t k) -> p t k", t=TILES) for a in (bank, out))
                    dve.scalar_tensor_tensor(out=out, in0=far, scalar=slope_now[:, e:e + 1], in1=bank,
                                             op0=ALU.mult, op1=ALU.add).then_inc(s_used, 1)
                    if before:
                        maxima(*before)
                    before = (n, e, c0, tiles)
                ins = maxima(*before)
                if g == N_GROUPS - 1:
                    ins.then_inc(mx_ready, 1)
                else:
                    ins.then_inc(dve_step, steps.add())

            def joint_maxima(i):
                dve.wait_ge(mx_in, i * (16 * 18) + 16 * 18)
                dve.tensor_reduce(joint[:, :].rearrange("p (g m) -> p g m", g=N_GROUPS),
                                  mall[:, :, :, :].rearrange("p g a m -> p g m a"), AX.X,
                                  ALU.max).then_inc(dve_step, steps.add())
                dve.wait_ge(dve_step, steps.count())
                dve.tensor_scalar(negm[:, :], joint[:, :], -1.0, None, ALU.mult).then_inc(negm_ready, 1)

            def pair(i, first):
                dve.tensor_copy(slope_now[:, :], cst[:, bass.ds(i * 2 + SLOPES, 2)]).then_inc(dve_step, steps.add())
                for q in range(PER_PAIR):
                    split(i * PER_PAIR + (ATT0 + q + AHEAD), (q + AHEAD) % RING_ATT)
                    p = i * PER_PAIR + (ATT0 + q)
                    dve.wait_ge(panel_done, p + (1 + CREDIT))
                    g = q // 2 if q < 6 else q - 6
                    to = (k_t, q_t)[q % 2][:, g, :] if q < 6 else v_t[:, g % 2, :]
                    bank = order(banks[q % RING_ATT][:, :], g)
                    if q in (1, 3, 5):
                        dve.scalar_tensor_tensor(out=grouped(to, g), in0=bank, scalar=HEAD ** -0.5,
                                                 in1=order(rstd[:, :], g), op0=ALU.mult,
                                                 op1=ALU.mult).then_inc(bank_free, 1)
                    else:
                        dve.tensor_tensor(grouped(to, g), bank, order(rstd[:, :], g), ALU.mult).then_inc(bank_free, 1)
                    if not first and q == 0:
                        copy_v(i - 1, 2)
                    if not first and q in ATTEND_AT:
                        combine(i - 1, ATTEND_AT.index(q))
                        if q == ATTEND_AT[-1]:
                            normalize(i - 1)
                    if q in SCORES_AT:
                        if q == SCORES_AT[0]:
                            dve.wait_ge(dve_step, steps.count())
                        score_pieces(i, SCORES_AT.index(q))
                    if q in TURN_AT:
                        copy_v(i, q - TURN_AT[0])
                joint_maxima(i)

            inverse_rms(2)
            dve.wait_ge(dst_ready, 16)
            pair(0, True)
            with dve.Fori(1, PAIRS) as i:
                steps.enter(i - 1, 7)
                pair(i, False)
                steps.leave(PAIRS - 1)
            last = PAIRS - 1
            for c in range(2):
                split(WO0 + c + AHEAD, c + AHEAD)
            copy_v(last, 2)
            dve.wait_ge(ohi_done, 1)
            lo_part(o_lo[:, 0:last, :], o_t[:, 0:last, :], o_hi[:, 0:last, :], o_ready)
            for g in range(N_GROUPS):
                combine(last, g)
            normalize(last)
            dve.wait_ge(ohi_done, 2)
            lo_part(o_lo[:, last, :], o_t[:, last, :], o_hi[:, last, :], o_ready)
            for c in range(RING):
                if c >= 2:
                    ahead(WO0, 0, c)
                dve.wait_ge(panel_done, WO0 + c + 1 + CREDIT)
                for s in range(2):
                    j = 2 * c + s
                    dve.tensor_tensor(h[:, j, :], h[:, j, :], banks[j][:, :], ALU.add).then_inc(h_ready, 1)
                    normed(xn_hi, xn_lo, GMLP1, j, xhi_done, X_MLP1 + j + 1, xn_ready)
            dve.sem_inc(bank_free, KC // 2)
            mlp(MLP1, Z_MLP1, 3, ())

            inverse_rms(4)
            for k in range(KC):
                dve.scalar_tensor_tensor(out=final[:, k, :], in0=h[:, k, :], scalar=cst[:, GFIN + k:GFIN + k + 1],
                                         in1=rstd[:, :], op0=ALU.mult, op1=ALU.mult).then_inc(out_ready, 1)

        @block.gpsimd
        def _(pool):
            pool.memset(ones[:, :], 1.0).then_inc(ones_ready, 1)
            pool.memset(cu[:, 0:2], 0.0).then_inc(ones_ready, 1)
            steps = Steps()

            def squares(n, chunk_ready):
                if n:
                    pool.wait_ge(ss_done, n)
                for k in range(KC):
                    pool.wait_ge(*chunk_ready(k))
                    if steps.count():
                        pool.wait_ge(sq_step, steps.count())
                    to = sq if k else sq_sum
                    pool.tensor_tensor(to[:, :], h[:, k, :], h[:, k, :], ALU.mult).then_inc(sq_step, steps.add())
                    if k:
                        pool.wait_ge(sq_step, steps.count())
                        ins = pool.tensor_tensor(sq_sum[:, :], sq_sum[:, :], sq[:, :], ALU.add)
                        if k < KC - 1:
                            ins.then_inc(sq_step, steps.add())
                        else:
                            ins.then_inc(sq_ready, 1)

            squares(0, lambda k: (x_ready[k], 16))
            squares(1, lambda k: (bank_free, OUT0 + k + 1 + CREDIT))
            squares(2, lambda k: (h_ready, k + 1))
            pool.wait_ge(panel_done, ATT0 + CREDIT)
            pool.memset(v_sb[:, :, :, HEAD:2 * HEAD], 1.0).then_inc(vones_ready, 1)
            squares(3, lambda k: (h_ready, KC + k + 1))
            squares(4, lambda k: (h_ready, 2 * KC + k + 1))


def build(nc, arrays):
    ins = {n: nc.dram_tensor(n, a.shape, F32, kind="ExternalInput").ap() for n, a in arrays.items()}
    out_t = nc.dram_tensor("out_t", (KC, P, SEQ), F32, kind="ExternalOutput").ap()
    scratch = nc.dram_tensor("scratch", (N_GROUPS, SEQ, 2), F32, kind="Internal").ap()
    yoco_trunk(nc, ins["x_t"], ins["weights"], ins["consts"], ins["dist"], ins["ident"], out_t, scratch)


def kernel(x, norm_mix, norm_mlp, w_a_in, conv_w, w_a_out, norm_kv, w_kv, w_q, w_o, w_up, w_down, norm_final):
    import numpy as np
    import concourse.bacc as bacc
    from concourse.bass_utils import run_bass_kernel_spmd

    f = np.float32
    x, norm_mix, norm_mlp, w_a_in, conv_w, w_a_out, norm_kv, w_kv, w_q, w_o, w_up, w_down, norm_final = (
        np.asarray(a) for a in (x, norm_mix, norm_mlp, w_a_in, conv_w, w_a_out, norm_kv, w_kv, w_q, w_o,
                                w_up, w_down, norm_final))

    def blocks(w, row, col, rows=D):
        return w[row:row + rows, col:col + P].reshape(rows // P, P, P).transpose(1, 0, 2)

    panels = []
    for j in range(KC):
        panels += [blocks(w_a_in[0], 0, part * D + j * P) for part in (1, 2, 0)]
    panels += [blocks(w_a_out[0], 0, j * P) for j in range(KC)]

    def mlp(layer):
        for half in range(2):
            for j in range(ZC):
                yield blocks(w_up[layer], 0, half * HALF + j * P)
            for j in range(KC):
                for part in range(2):
                    yield blocks(w_down[layer], half * HALF + part * D, j * P)

    panels += mlp(0)
    width = H_G * HEAD
    for pair in range(PAIRS):
        for g in range(N_GROUPS):
            panels += [blocks(w_kv, 0, g * 2 * width + pair * P), blocks(w_q[0], 0, g * width + pair * P)]
        panels += [blocks(w_kv, 0, (g * 2 + 1) * width + pair * P) for g in range(N_GROUPS)]
    for j in range(0, KC, 2):
        panels.append(np.concatenate([blocks(w_o[0], 0, (j + s) * P, width) for s in range(2)], axis=1))
    panels += mlp(1)

    consts = np.zeros((P, N_CONST), f)
    gains = (norm_mix[0], norm_mlp[0], norm_kv, norm_mix[1], norm_mlp[1], norm_final)
    for n, gain in enumerate(gains + tuple(conv_w[0])):
        consts[:, n * KC:(n + 1) * KC] = gain.reshape(KC, P).T
    consts[:, SLOPES:SLOPES + H_G] = [-(2.0 ** -(n + 1)) for n in range(H_G)]
    consts[:, EPSC] = EPS

    a, c = np.arange(P)[:, None], np.arange(P)[None, :]
    own = np.where(c <= a, a - c, MASKED).astype(f)
    prev = np.where(c >= a, P + a - c, MASKED).astype(f)
    n2 = SEQ // DILATIONS[2]
    dist = np.concatenate([own, prev, own, prev, own, np.where(c <= a, DILATIONS[1] * (a - c), MASKED),
                           np.where((c <= a) & (a // n2 == c // n2),
                                    DILATIONS[2] * (a - c), MASKED)], axis=1).astype(f)

    arrays = {
        "x_t": np.ascontiguousarray(x[0].T.reshape(KC, P, SEQ)),
        "weights": np.stack([p.reshape(P, PANEL) for p in panels]),
        "consts": consts, "dist": dist, "ident": np.eye(P, dtype=f),
    }
    nc = bacc.Bacc("TRN2", target_bir_lowering=False, num_devices=1)
    build(nc, arrays)
    r = run_bass_kernel_spmd(nc, [arrays], core_ids=[0])
    return r.results[0]["out_t"].reshape(D, SEQ).T[None]
```

```python
from contextlib import ExitStack

import concourse.bass as bass
from concourse import mybir

F32 = mybir.dt.float32
F32R = mybir.dt.float32r
ALU = mybir.AluOpType
ACT = mybir.ActivationFunctionType
AX = mybir.AxisListType

P = 128
SEQ = 512
D = 1024
KC = D // P
FF = 4 * D
HALF = FF // 2
ZC = HALF // P
N_GROUPS, H_G, HEAD = 3, 8, 64
PAIRS = H_G // 2
DILATIONS = (1, 4, 16)
TILES = SEQ // P
EPS = 1e-5
MASKED = 2.0 ** 126

PANEL = KC * P
RING = 4
RING_ATT = 3
CREDIT = RING
PER_PAIR = 3 * N_GROUPS

IN0 = 0
OUT0 = IN0 + 3 * KC
MLP0 = OUT0 + KC
HALF_PANELS = ZC + 2 * KC
ATT0 = MLP0 + 2 * HALF_PANELS
WO0 = ATT0 + PAIRS * PER_PAIR
MLP1 = WO0 + KC // 2
N_PANELS = MLP1 + 2 * HALF_PANELS
assert IN0 % RING == OUT0 % RING == MLP0 % RING == ATT0 % RING == WO0 % RING == MLP1 % RING == 0

MIX0, GMLP0, GKV, MIX1, GMLP1, GFIN = (n * KC for n in range(6))
TAPS = 6 * KC
SLOPES = TAPS + 3 * KC
EPSC = SLOPES + H_G
N_CONST = EPSC + 1

SC0, SC1, SC2 = 0, 7 * P, 11 * P
SCORES = 15 * P
SC = (SC0, SC1, SC2)
TILE_COLS = (
    ((0, P), (P, 3 * P), (3 * P, 5 * P), (5 * P, 7 * P)),
    tuple((SC1 + t * P, SC1 + (t + 1) * P) for t in range(TILES)),
    tuple((SC2 + t * P, SC2 + (t + 1) * P) for t in range(TILES)),
)
PIECES = (
    tuple((e, c, tiles) for e in range(2)
          for c, tiles in ((0, ((0, 0, 1), (1, 0, 2))), (3 * P, ((2, 1, 2), (3, 2, 2))))),
    tuple((e, SC1, tuple((t, t, 1) for t in range(TILES))) for e in range(2)),
    tuple((e, SC2, tuple((t, t, 1) for t in range(TILES))) for e in range(2)),
)
PIECE0, ROWS_PIECE, BACK_PIECE, N_PIECES = (0, 5, 8), (4, 7, 10), 11, 12
LOTS = ((0, 0, 0, 4), (0, 0, 4, 3), (0, 1, 0, 4), (0, 1, 4, 3), (1, 0, 0, 4), (1, 1, 0, 4), (2, 0, 0, 4), (2, 1, 0, 4))
UNITS = ((0, 0, (0, 1)), (0, 1, (2, 3)), (1, 0, (4,)), (1, 1, (5,)), (2, 0, (6,)), (2, 1, (7,)))
AFTER = (
    ((True, "turn_v", 2), (True, "turn_p", 0), (True, "turn_p", 1)),
    ((True, "turn_p", 2), (True, "turn_p", 3), (True, "attend", 0)),
    ((True, "attend", 1), (False, "scores", 0)),
    ((True, "turn_p", 4), (True, "turn_p", 5), (False, "rows", 0)),
    ((True, "attend", 2), (True, "turn_p", 6), (True, "turn_p", 7), (False, "scores", 1)),
    ((True, "attend", 3), (False, "rows", 1)),
    ((True, "attend", 4), (False, "scores", 2)),
    ((True, "attend", 5), (False, "rows", 2), (False, "turn_v", 0)),
    ((False, "back", 0), (False, "turn_v", 1)),
)
MAXES = N_GROUPS * TILES * 2


class Steps:

    def __init__(self):
        self.before, self.here, self.turn, self.per = 0, 0, 0, 0

    def add(self):
        self.here += 1
        return 1

    def count(self):
        return self.turn * self.per + (self.before + self.here) if self.per else self.before + self.here

    def enter(self, turn, per):
        self.before, self.here, self.turn, self.per = self.before + self.here, 0, turn, per

    def leave(self, turns):
        assert self.here == self.per, (self.here, self.per)
        self.before, self.here, self.turn, self.per = self.before + turns * self.per, 0, 0, 0


def yoco_trunk(nc, x_t, weights, consts, dist, ident, out_t):
    ctx = ExitStack()
    with ctx:
        base = (nc.sbuf_base + 63) // 64 * 64
        slab = ctx.enter_context(nc.sbuf_tensor("slab", [P, (nc.sbuf_usable_end - base - 128) // 4], F32))
        at = [base]
        end = nc.sbuf_usable_end - 64

        def place(name, shape, dt, offset=None):
            size = 4
            for n in shape:
                size *= n
            where = at[0] if offset is None else offset
            if offset is None:
                at[0] += (size + 31) // 32 * 32
                assert at[0] <= end, (name, at[0] - end)
            t = nc.alloc_sbuf_tensor_at(name, [P, *shape], dtype=dt, offset=where)
            return t, where + (size + 31) // 32 * 32

        h, _ = place("h", [KC, SEQ], F32)
        xn_hi, _ = place("xn_hi", [KC, SEQ], F32R)
        xn_lo, _ = place("xn_lo", [KC, SEQ], F32R)
        kv_area = at[0]
        xkv_hi, _ = place("xkv_hi", [KC, SEQ], F32R)
        xkv_lo, _ = place("xkv_lo", [KC, SEQ], F32R)
        z_area = at[0]
        z_hi, _ = place("z_hi", [ZC, SEQ], F32R)
        z_lo, z_end = place("z_lo", [ZC, SEQ], F32R)
        w_raw, _ = place("w_raw", [RING, PANEL], F32)
        w_hi, _ = place("w_hi", [RING, PANEL], F32R)
        w_lo, _ = place("w_lo", [RING, PANEL], F32R)
        rstd, _ = place("rstd", [SEQ], F32)
        rstd2, _ = place("rstd2", [SEQ], F32)
        sq_area = at[0]
        sq_sum, _ = place("sq_sum", [SEQ], F32)
        sq, _ = place("sq", [SEQ], F32)
        tmp, _ = place("tmp", [2, SEQ], F32)
        tmp2, _ = place("tmp2", [SEQ], F32)
        cst, _ = place("cst", [N_CONST], F32)
        ones, _ = place("ones", [P], F32)
        idn, _ = place("idn", [P], F32)
        ms4, _ = place("ms4", [TILES], F32)
        root4, _ = place("root4", [TILES], F32)
        cu, nxt = place("cu", [SEQ + 2], F32, kv_area)
        conv, nxt = place("conv", [3, SEQ], F32, nxt)
        gate, nxt = place("gate", [SEQ], F32, nxt)
        mixed, nxt = place("mixed", [SEQ], F32, nxt)
        final, _ = place("final", [KC, SEQ], F32, kv_area)
        o_hi, nxt = place("o_hi", [PAIRS, SEQ], F32R, kv_area)
        o_lo, _ = place("o_lo", [PAIRS, SEQ], F32R, nxt)
        k_t, nxt = place("k_t", [N_GROUPS, SEQ], F32, z_area)
        q_t, nxt = place("q_t", [N_GROUPS, SEQ], F32, nxt)
        sc, nxt = place("sc", [2, SCORES], F32, nxt)
        p_t, nxt = place("p_t", [4, SEQ], F32, nxt)
        v_sb, nxt = place("v_sb", [N_GROUPS, TILES, 3 * HEAD], F32, nxt)
        v_t, nxt = place("v_t", [2, SEQ], F32, nxt)
        dst, nxt = place("dst", [7 * P], F32, nxt)
        rec, nxt = place("rec", [SEQ], F32, nxt)
        o_t, nxt = place("o_t", [PAIRS, SEQ], F32, nxt)
        mx, nxt = place("mx", [MAXES], F32, nxt)
        negm, nxt = place("negm", [MAXES], F32, nxt)
        slope_now, nxt = place("slope_now", [2], F32, nxt)
        assert nxt <= z_end, nxt - z_end
        rows, _ = place("rows", [2, SEQ], F32, sq_area)
        acc = tmp

        banks = [ctx.enter_context(nc.psum_tensor(f"bank{n}", [P, SEQ], F32)) for n in range(8)]
        STAT = O_BANK = 7
        S_BANK, T_BANK = 3, 5

        def sem(name):
            return ctx.enter_context(nc.semaphore(name))

        raw_ready = [sem(f"raw_ready{n}") for n in range(RING)]
        x_ready = [sem(f"x_ready{n}") for n in range(KC)]
        cst_ready, idn_ready, dst_ready = sem("cst_ready"), sem("idn_ready"), sem("dst_ready")
        ones_ready = sem("ones_ready")
        vones_ready = sem("vones_ready")
        hi_done = sem("hi_done")
        lo_done = sem("lo_done")
        panel_done = sem("panel_done")
        bank_free = sem("bank_free")
        xhi_done = sem("xhi_done")
        kvhi_done = sem("kvhi_done")
        zhi_done = sem("zhi_done")
        ohi_done = sem("ohi_done")
        xn_ready, xkv_ready = sem("xn_ready"), sem("xkv_ready")
        z_ready, o_ready = sem("z_ready"), sem("o_ready")
        r_done = sem("r_done")
        mixed_ready = sem("mixed_ready")
        h_ready = sem("h_ready")
        sq_step = sem("sq_step")
        sq_ready = sem("sq_ready")
        ss_done = sem("ss_done")
        std_done = sem("std_done")
        inv_ready = sem("inv_ready")
        inv_spread = sem("inv_spread")
        x_squares = sem("x_squares")
        last_square = sem("last_square")
        dve_step = sem("dve_step")
        s_done, s_used = sem("s_done"), sem("s_used")
        mx_ready = sem("mx_ready")
        p_ready = sem("p_ready")
        t_done, t_used = sem("t_done"), sem("t_used")
        ob_filled, ob_free = sem("ob_filled"), sem("ob_free")
        ot_ready = sem("ot_ready")
        out_ready, out_done = sem("out_ready"), sem("out_done")

        X_IN, X_MLP0, X_MIX1, X_MLP1 = 0, KC, 2 * KC, 3 * KC
        Z_Y, Z_MLP0, Z_MLP1 = 0, KC, KC + 2 * ZC

        def order(ap, group):
            r = DILATIONS[group]
            return ap if r == 1 else ap.rearrange("p (i r) -> p r i", r=r)

        def grouped(ap, group):
            r = DILATIONS[group]
            return ap if r == 1 else ap.rearrange("p (r i) -> p r i", r=r)

        def landed(phase, slot):
            fills = min(phase, ATT0) // RING
            if phase > ATT0:
                fills += (PAIRS * PER_PAIR // RING_ATT if slot < RING_ATT else 0) + (phase - WO0) // RING
            return fills

        block = ctx.enter_context(nc.Block())

        @block.sync
        def _(sp):
            def load(p, slot, ring=RING):
                sp.wait_ge(lo_done, p + (1 - ring + CREDIT))
                sp.dma_start(w_raw[:, slot, :], weights[p]).then_inc(raw_ready[slot], 16)

            sp.dma_start(cst[:, :], consts).then_inc(cst_ready, 16)
            load(0, 0)
            for k in range(KC):
                sp.dma_start(h[:, k, :], x_t[k]).then_inc(x_ready[k], 16)
            for p in range(1, RING):
                load(p, p)
            sp.dma_start(idn[:, :], ident).then_inc(idn_ready, 16)
            with sp.Fori(1, ATT0 // RING) as i:
                for c in range(RING):
                    load(i * RING + c, c)
            for q in range(RING_ATT):
                load(ATT0 + q, q, RING_ATT)
            sp.wait_ge(panel_done, ATT0 + CREDIT)
            sp.dma_start(dst[:, :], dist).then_inc(dst_ready, 16)
            with sp.Fori(0, PAIRS) as i:
                for q in range(PER_PAIR):
                    load(i * PER_PAIR + (ATT0 + RING_ATT + q), q % RING_ATT, RING_ATT)
            load(MLP1 - 1, RING - 1)
            with sp.Fori(MLP1 // RING, N_PANELS // RING) as i:
                for c in range(RING):
                    load(i * RING + c, c)
            for k in range(KC):
                sp.wait_ge(out_ready, k + 1)
                sp.dma_start(out_t[k], final[:, k, :]).then_inc(out_done, 16)
            sp.wait_ge(out_done, 16 * KC)

        @block.tensor
        def _(pe):
            pe.sem_inc(panel_done, CREDIT)

            def products(out, slot, col, hi, lo, chunks, first, last, ready=None):
                for n, k in enumerate(chunks):
                    if ready is not None:
                        pe.wait_ge(ready[0], ready[1] + k + 1)
                    w = slice(col + n * P, col + (n + 1) * P)
                    pe.matmul(out, w_hi[:, slot, w], hi[:, k, :], start=first and n == 0, stop=False)
                    pe.matmul(out, w_hi[:, slot, w], lo[:, k, :], start=False, stop=False)
                    mm = pe.matmul(out, w_lo[:, slot, w], hi[:, k, :], start=False,
                                   stop=last and n == len(chunks) - 1)
                return mm

            def panel(p, slot, bank, hi, lo, chunks=range(KC), first=True, last=True, ready=None, ring=RING):
                pe.wait_ge(lo_done, p + (1 + CREDIT))
                if first:
                    pe.wait_ge(bank_free, p + (1 - ring + CREDIT))
                products(banks[bank][:, :], slot, 0, hi, lo, chunks, first, last, ready).then_inc(panel_done, 1)

            def stats(n, last_apart=False):
                pe.wait_ge(sq_ready, n + 1)
                if last_apart:
                    pe.wait_ge(last_square, 1 if n == 2 else 2)
                for t in range(TILES):
                    tile = slice(t * P, (t + 1) * P)
                    mm = pe.matmul(banks[STAT][:, t:t + 1], sq_sum[:, tile], ones[:, 0:1], start=True,
                                   stop=not last_apart)
                    if last_apart:
                        mm = pe.matmul(banks[STAT][:, t:t + 1], tmp[:, 0, tile], ones[:, 0:1], start=False, stop=True)
                mm.then_inc(ss_done, 1)

            def spread(n):
                pe.wait_ge(inv_ready, n + 1)
                for t in range(TILES):
                    mm = pe.matmul(banks[STAT][:, t * P:(t + 1) * P], root4[:, t:t + 1].broadcast_to([P, P]),
                                   idn[:, :], start=True, stop=True)
                mm.then_inc(inv_spread, 1)

            def mlp(p0, x_count, z_count, norm):
                for half in range(2):
                    up, down = p0 + half * HALF_PANELS, p0 + half * HALF_PANELS + ZC
                    rounds = ZC // RING
                    with pe.Fori(0, rounds - (half == 0)) as i:
                        for c in range(RING):
                            panel(i * RING + (up + c), c, c, xn_hi, xn_lo,
                                  ready=(xn_ready, x_count) if c == 0 else None)
                    if half == 0:
                        stats(norm)
                        for c in range(RING):
                            panel(up + (rounds - 1) * RING + c, c, c, xn_hi, xn_lo)
                        spread(norm)
                    with pe.Fori(0, 2 * KC // 8) as i:
                        for c in range(8):
                            k0 = KC * (c % 2)
                            panel(i * 8 + (down + c), c % RING, c // 2, z_hi, z_lo, chunks=range(k0, k0 + KC),
                                  first=c % 2 == 0, last=c % 2 == 1,
                                  ready=(z_ready, z_count + half * ZC) if c < 2 else None)

            pe.wait_ge(ones_ready, 1)
            for c in range(RING):
                panel(IN0 + c, c, c, xn_hi, xn_lo, ready=(xn_ready, X_IN) if c == 0 else None)
                if c == 1:
                    stats(0)
                if c == 2:
                    pe.wait_ge(idn_ready, 16)
                    spread(0)
            with pe.Fori(1, 3 * KC // RING) as i:
                for c in range(RING):
                    panel(i * RING + (IN0 + c), c, c, xn_hi, xn_lo)
            with pe.Fori(0, KC // RING) as i:
                for c in range(RING):
                    panel(i * RING + (OUT0 + c), c, c, z_hi, z_lo, ready=(z_ready, Z_Y) if c == 0 else None)
            mlp(MLP0, X_MLP0, Z_MLP0, 1)

            def scores(i, g):
                pe.wait_ge(bank_free, i * PER_PAIR + (ATT0 + 2 * g + 2 + CREDIT))
                for n, (e, _, tiles) in enumerate(PIECES[g]):
                    n += PIECE0[g]
                    pe.wait_ge(s_used, i * N_PIECES + (n + 1))
                    heads = slice(HEAD * e, HEAD * e + HEAD)
                    bank, col = banks[S_BANK + n % 2], 0
                    for tile, key, nk in tiles:
                        mm = pe.matmul(bank[:, col:col + nk * P], q_t[heads, g, tile * P:(tile + 1) * P],
                                       k_t[heads, g, key * P:(key + nk) * P], start=True, stop=True)
                        col += nk * P
                    mm.then_inc(s_done, 1)

            def turn_maxima(i, g):
                n = ROWS_PIECE[g]
                pe.wait_ge(mx_ready, i * N_GROUPS + (g + 1))
                pe.wait_ge(s_used, i * N_PIECES + (n + 1))
                for t in range(TILES):
                    m = (g * TILES + t) * 2
                    mm = pe.transpose(banks[S_BANK + n % 2][0:2, t * P:(t + 1) * P], mx[:, m:m + 2], idn[:, :])
                mm.then_inc(s_done, 1)

            def maxima_back(i):
                n = BACK_PIECE
                pe.wait_ge(s_used, i * N_PIECES + (n + 2))
                for g in range(N_GROUPS):
                    for t in range(TILES):
                        m = (g * TILES + t) * 2
                        if g == 1:
                            tokens = rows[0:2, 0, t:SEQ:TILES]
                        else:
                            tokens = rows[0:2, g // 2, t * P:(t + 1) * P]
                        mm = pe.matmul(banks[S_BANK + n % 2][:, m:m + 2], tokens, idn[0:2, 0:2], start=True, stop=True)
                mm.then_inc(s_done, 1)

            def turn_v(i, g):
                pe.wait_ge(bank_free, i * PER_PAIR + (ATT0 + 6 + g + 1 + CREDIT))
                pe.wait_ge(ob_free, i * 9 + (g + 1))
                for t in range(TILES):
                    mm = pe.transpose(banks[O_BANK][:, t * P:(t + 1) * P], v_t[:, g % 2, t * P:(t + 1) * P],
                                      idn[:, :])
                mm.then_inc(ob_filled, 1)

            def turn_p(i, n):
                g, e, tile, nt = LOTS[n]
                pe.wait_ge(p_ready, i * N_GROUPS + (g + 1))
                pe.wait_ge(t_used, i * 8 + (n + 1))
                for t in range(nt):
                    c = SC[g] + (tile + t) * P
                    mm = pe.transpose(banks[T_BANK + n % 2][:, t * P:(t + 1) * P], sc[:, e, c:c + P], idn[:, :])
                mm.then_inc(t_done, 1)

            def attend(i, unit):
                g, e, lots = UNITS[unit]
                out, vcols = banks[O_BANK], slice(HEAD * e, HEAD * e + P)
                pe.wait_ge(ob_free, i * 9 + (4 + unit))
                for n in lots:
                    pe.wait_ge(t_used, i * 8 + (n + 3))
                    tile = LOTS[n][2]
                    if g == 0:
                        for key in (tile // 2, tile // 2 + 1):
                            nq = min(2, TILES - key)
                            c = (2 * key - tile) * P
                            mm = pe.matmul(out[:, key * P:(key + nq) * P], v_sb[:, g, key, vcols],
                                           p_t[:, n % 4, c:c + nq * P], start=key == 0,
                                           stop=key == TILES - 1, skip_group_check=True)
                    else:
                        for t in range(TILES):
                            mm = pe.matmul(out[:, t * P:(t + 1) * P], v_sb[:, g, t, vcols],
                                           p_t[:, n % 4, t * P:(t + 1) * P], start=True, stop=True)
                mm.then_inc(ob_filled, 1)

            def pair(i, first):
                for q in range(PER_PAIR):
                    hi, lo = (xn_hi, xn_lo) if q in (1, 3, 5) else (xkv_hi, xkv_lo)
                    ready = ((xkv_ready, 0), (xn_ready, X_MIX1))[q] if first and q < 2 else None
                    panel(i * PER_PAIR + (ATT0 + q), q % RING_ATT, q % RING_ATT, hi, lo, ready=ready,
                          ring=RING_ATT)
                    if first and q == 0:
                        stats(2, last_apart=True)
                    if first and q == 1:
                        spread(2)
                    for before, what, n in AFTER[q]:
                        if before and first:
                            continue
                        j = i - 1 if before else i
                        if what == "scores":
                            scores(j, n)
                        elif what == "rows":
                            turn_maxima(j, n)
                        elif what == "back":
                            maxima_back(j)
                        elif what == "turn_v":
                            turn_v(j, n)
                        elif what == "turn_p":
                            turn_p(j, n)
                        else:
                            attend(j, n)

            pair(0, True)
            pe.wait_ge(vones_ready, 1)
            with pe.Fori(1, PAIRS) as i:
                pair(i, False)

            last = PAIRS - 1

            def out_part(j, chunks):
                c, first = (j % 2 * PAIRS + chunks[0]) * P, chunks[0] == 0
                return products(banks[j][:, :], j // 2, c, o_hi, o_lo, chunks, first, chunks[-1] == last)

            turn_v(last, 2)
            pe.wait_ge(bank_free, WO0 + CREDIT)
            pe.wait_ge(s_used, N_PIECES * PAIRS + 2)
            pe.wait_ge(o_ready, 1)
            pe.wait_ge(lo_done, WO0 + 2 + CREDIT)
            for j in range(4):
                out_part(j, range(last))
            turn_p(last, 0)
            turn_p(last, 1)
            turn_p(last, 2)
            attend(last, 0)
            turn_p(last, 3)
            turn_p(last, 4)
            attend(last, 1)
            turn_p(last, 5)
            turn_p(last, 6)
            attend(last, 2)
            turn_p(last, 7)
            pe.wait_ge(lo_done, WO0 + 4 + CREDIT)
            attend(last, 3)
            attend(last, 4)
            out_part(4, range(last))
            attend(last, 5)
            pe.wait_ge(t_used, 8 * PAIRS + 2)
            out_part(5, range(last))
            out_part(6, range(last))
            pe.wait_ge(o_ready, 2)
            for j in range(KC):
                mm = out_part(j, range(last, PAIRS) if j < KC - 1 else range(PAIRS))
                if j % 2:
                    mm.then_inc(panel_done, 1)
            mlp(MLP1, X_MLP1, Z_MLP1, 3)
            stats(4, last_apart=True)
            spread(4)

        @block.scalar
        def _(act):
            act.sem_inc(t_used, 2)

            def split(p, slot, fills, ring=RING):
                act.wait_ge(raw_ready[slot], fills * 16)
                act.wait_ge(panel_done, p + (1 - ring + CREDIT))
                act.copy(w_hi[:, slot, :], w_raw[:, slot, :]).then_inc(hi_done, 1)

            def ahead(phase, turn, c, rings=1):
                slot = c % RING
                split(turn * (rings * RING) + (phase + c + RING), slot,
                      turn * rings + (landed(phase, slot) + 2 + c // RING))

            def normed(hi, gain, j, done):
                act.activation(hi[:, j, :], h[:, j, :], ACT.Copy, scale=cst[:, bass.ds(j + gain, 1)]).then_inc(done, 1)

            def root(n):
                act.wait_ge(ss_done, n + 1)
                act.activation(root4[:, :], banks[STAT][:, 0:TILES], ACT.Sqrt, scale=1.0 / D,
                               bias=cst[:, EPSC:EPSC + 1]).then_inc(std_done, 1)

            def mlp(p0, z_count, norm, h_count, gains):
                for half in range(2):
                    up, down = p0 + half * HALF_PANELS, p0 + half * HALF_PANELS + ZC
                    relus = half * ZC + (0 if p0 == MLP0 else 2 * ZC)
                    rounds = ZC // RING

                    def up_turn(i):
                        for c in range(RING):
                            p = i * RING + (up + c)
                            act.wait_ge(bank_free, p + (1 - 2 + CREDIT))
                            act.wait_ge(panel_done, p + (1 + CREDIT))
                            act.activation(tmp[:, c % 2, :], banks[c][:, :], ACT.Relu).then_inc(r_done, 1)
                            act.wait_ge(r_done, i * RING + (relus + c + 1))
                            act.activation(z_hi[:, i * RING + c, :], tmp[:, c % 2, :], ACT.Square).then_inc(zhi_done, 1)
                            ahead(up, i, c)

                    with act.Fori(0, rounds - (half == 0)) as i:
                        up_turn(i)
                    if half == 0:
                        root(norm)
                        up_turn(rounds - 1)

                    def down_turn(i, following=True):
                        for c in range(2 * RING):
                            if half == 1 and c % 2 == 1:
                                if gains:
                                    act.wait_ge(h_ready, i * RING + (h_count + c // 2 + 1))
                                    for hi, gain, done in gains:
                                        normed(hi, gain, i * RING + c // 2, done)
                            if following or (c < RING or p0 == MLP0 and c < 2 * RING - 1):
                                ahead(down, i, c, 2)

                    if half == 0:
                        with act.Fori(0, 2) as i:
                            down_turn(i)
                    else:
                        down_turn(0)
                        down_turn(1, following=False)
                        act.wait_ge(h_ready, h_count + KC)
                        act.activation(tmp[:, 0, :], h[:, KC - 1, :], ACT.Square).then_inc(last_square, 1)

            act.wait_ge(cst_ready, 16)
            split(0, 0, 1)
            for k in range(KC):
                act.wait_ge(x_ready[k], 16)
                normed(xn_hi, MIX0, k, xhi_done)
            for c in range(1, RING):
                split(c, c, 1)
            root(0)
            with act.Fori(0, KC // RING) as i:
                for c in range(3 * RING):
                    if c % 3 == 2:
                        act.wait_ge(mixed_ready, i * RING + (c // 3 + 1))
                        act.copy(z_hi[:, i * RING + c // 3, :], mixed[:, :]).then_inc(zhi_done, 1)
                    ahead(IN0, i, c, 3)
            with act.Fori(0, KC // RING) as i:
                for c in range(RING):
                    act.wait_ge(bank_free, i * RING + (OUT0 + c + 1 + CREDIT))
                    normed(xn_hi, GMLP0, i * RING + c, xhi_done)
                    ahead(OUT0, i, c)
            mlp(MLP0, Z_MLP0, 1, 0, ((xn_hi, MIX1, xhi_done), (xkv_hi, GKV, kvhi_done)))

            def exps(i, g):
                act.wait_ge(s_used, i * N_PIECES + (BACK_PIECE + 3))
                for e in range(2):
                    for t in range(TILES):
                        cols = slice(*TILE_COLS[g][t])
                        m = (g * TILES + t) * 2 + e
                        ins = act.activation(sc[:, e, cols], sc[:, e, cols], ACT.Exp, bias=negm[:, m:m + 1])
                ins.then_inc(p_ready, 1)

            def copy_lot(i, n):
                nt = LOTS[n][3]
                act.wait_ge(t_done, i * 8 + (n + 1))
                act.wait_ge(ob_filled, i * 9 + (3 if n < 4 else 4 + (n - 4) // 2))
                act.copy(p_t[:, n % 4, 0:nt * P], banks[T_BANK + n % 2][:, 0:nt * P]).then_inc(t_used, 1)

            def pair(i, first):
                for q in range(PER_PAIR):
                    if not first:
                        if q < N_GROUPS:
                            exps(i - 1, q)
                        for _, what, n in AFTER[q]:
                            if what == "turn_p":
                                copy_lot(i - 1, n)
                    slot = q % RING_ATT
                    split(i * PER_PAIR + (ATT0 + q + RING_ATT), slot,
                          i * (PER_PAIR // RING_ATT) + (landed(ATT0, slot) + q // RING_ATT + 2), RING_ATT)

            root(2)
            pair(0, True)
            with act.Fori(1, PAIRS) as i:
                pair(i, False)
            last = PAIRS - 1
            act.wait_ge(panel_done, WO0 + CREDIT)
            act.wait_ge(ot_ready, last)
            act.copy(o_hi[:, 0:last, :], o_t[:, 0:last, :]).then_inc(ohi_done, 1)
            exps(last, 0)
            exps(last, 1)
            for n in range(4):
                copy_lot(last, n)
            exps(last, 2)
            for n in range(4, 6):
                copy_lot(last, n)
            split(MLP1 - 1, RING - 1, landed(MLP1 - 1, RING - 1) + 1)
            for n in range(6, 8):
                copy_lot(last, n)
            act.wait_ge(ot_ready, PAIRS)
            act.copy(o_hi[:, last, :], o_t[:, last, :]).then_inc(ohi_done, 1)
            for c in range(RING):
                for s in range(2):
                    act.wait_ge(h_ready, KC + 2 * c + s + 1)
                    normed(xn_hi, GMLP1, 2 * c + s, xhi_done)
                ahead(WO0, 0, c)
            mlp(MLP1, Z_MLP1, 3, 2 * KC, ())
            root(4)

        @block.vector
        def _(dve):
            dve.sem_inc(lo_done, CREDIT)
            dve.sem_inc(bank_free, CREDIT)
            dve.sem_inc(s_used, 2)
            dve.sem_inc(ob_free, 1)
            steps = Steps()

            def lo_part(lo, x, hi, done):
                dve.tensor_tensor(lo, x, hi.bitcast(F32), ALU.subtract).then_inc(done, 1)

            def split(p, slot):
                dve.wait_ge(hi_done, p + 1)
                lo_part(w_lo[:, slot, :], w_raw[:, slot, :], w_hi[:, slot, :], lo_done)

            def ahead(phase, turn, c, rings=1):
                split(turn * (rings * RING) + (phase + c + RING), c % RING)

            def normed(hi, lo, gain, j, counted, count, done):
                dve.wait_ge(counted, count)
                dve.scalar_tensor_tensor(out=lo[:, j, :], in0=h[:, j, :], scalar=cst[:, bass.ds(j + gain, 1)],
                                         in1=hi[:, j, :].bitcast(F32), op0=ALU.mult,
                                         op1=ALU.subtract).then_inc(done, 1)

            def inverse_rms(n):
                def step(ins):
                    ins.then_inc(dve_step, steps.add())
                    dve.wait_ge(dve_step, steps.count())
                dve.wait_ge(std_done, n + 1)
                dve.tensor_scalar(ms4[:, :], banks[STAT][:, 0:TILES], 1.0 / D, EPS, ALU.mult,
                                  ALU.add).then_inc(dve_step, steps.add())
                step(dve.reciprocal(root4[:, :], root4[:, :]))
                step(dve.tensor_tensor(ms4[:, :], ms4[:, :], root4[:, :], ALU.mult))
                step(dve.tensor_tensor(ms4[:, :], ms4[:, :], root4[:, :], ALU.mult))
                step(dve.tensor_scalar(ms4[:, :], ms4[:, :], -0.5, 1.5, ALU.mult, ALU.add))
                dve.tensor_tensor(root4[:, :], root4[:, :], ms4[:, :], ALU.mult).then_inc(inv_ready, 1)

            def take_rstd(n):
                dve.wait_ge(inv_spread, n + 1)
                dve.tensor_copy(rstd[:, :], banks[STAT][:, :]).then_inc(dve_step, steps.add())
                dve.wait_ge(dve_step, steps.count())
                dve.tensor_tensor(rstd2[:, :], rstd[:, :], rstd[:, :], ALU.mult).then_inc(dve_step, steps.add())
                dve.wait_ge(dve_step, steps.count())

            def mlp(p0, z_count, norm, gains):
                for half in range(2):
                    up, down = p0 + half * HALF_PANELS, p0 + half * HALF_PANELS + ZC
                    relus = half * ZC + (0 if p0 == MLP0 else 2 * ZC)
                    rounds = ZC // RING

                    def up_panel(i, c):
                        dve.wait_ge(z_ready, i * RING + (z_count + half * ZC + c))
                        dve.wait_ge(r_done, i * RING + (relus + c + 1))
                        dve.tensor_tensor(tmp2[:, :], tmp[:, c % 2, :], tmp[:, c % 2, :],
                                          ALU.mult).then_inc(bank_free, 1)
                        dve.wait_ge(bank_free, i * RING + (up + c + 1 + CREDIT))
                        dve.wait_ge(zhi_done, i * RING + (z_count + half * ZC + c + 1))
                        lo_part(z_lo[:, i * RING + c, :], tmp2[:, :], z_hi[:, i * RING + c, :], z_ready)
                        ahead(up, i, c)

                    with dve.Fori(0, rounds - (half == 0)) as i:
                        for c in range(RING):
                            up_panel(i, c)
                    if half == 0:
                        for c in range(RING):
                            up_panel(rounds - 1, c)
                            if c == 0:
                                inverse_rms(norm)
                        take_rstd(norm)
                    dve.wait_ge(z_ready, z_count + (half + 1) * ZC)

                    def down_turn(i, following=True):
                        for c in range(2 * RING):
                            if c % 2 == 1:
                                dve.wait_ge(dve_step, steps.count())
                                j, p = i * RING + c // 2, i * 2 * RING + (down + c)
                                dve.wait_ge(panel_done, p + (1 + CREDIT))
                                dve.tensor_tensor(tmp2[:, :], banks[c // 2][:, :], rstd2[:, :],
                                                  ALU.mult).then_inc(bank_free, 2)
                                dve.wait_ge(bank_free, p + (1 + CREDIT))
                                ins = dve.tensor_tensor(h[:, j, :], h[:, j, :], tmp2[:, :], ALU.add)
                                if half == 0:
                                    ins.then_inc(dve_step, steps.add())
                                else:
                                    ins.then_inc(h_ready, 1)
                                    dve.wait_ge(h_ready, j + ((0 if p0 == MLP0 else 2 * KC) + 1))
                                    for hi, lo, gain, counted, count, done in gains:
                                        normed(hi, lo, gain, j, counted, j + (count + 1), done)
                            if following or (c < RING or p0 == MLP0 and c < 2 * RING - 1):
                                ahead(down, i, c, 2)

                    if half == 0:
                        with dve.Fori(0, 2) as i:
                            steps.enter(i, RING)
                            down_turn(i)
                            steps.leave(2)
                        dve.wait_ge(dve_step, steps.count())
                    else:
                        down_turn(0)
                        down_turn(1, following=False)

            dve.wait_ge(cst_ready, 16)
            split(0, 0)
            for k in range(KC):
                normed(xn_hi, xn_lo, MIX0, k, xhi_done, X_IN + k + 1, xn_ready)
            split(1, 1)
            for k in range(KC // 2, KC):
                first = k == KC // 2
                dve.wait_ge(x_ready[k], 16)
                dve.tensor_tensor(tmp2[:, :] if first else tmp[:, k % 2, :], h[:, k, :], h[:, k, :],
                                  ALU.mult).then_inc(dve_step, steps.add())
                if not first:
                    dve.wait_ge(dve_step, steps.count())
                    dve.tensor_tensor(tmp2[:, :], tmp2[:, :], tmp[:, k % 2, :],
                                      ALU.add).then_inc(dve_step, steps.add())
            dve.wait_ge(dve_step, steps.count())
            dve.wait_ge(x_squares, 1)
            dve.tensor_tensor(sq_sum[:, :], sq_sum[:, :], tmp2[:, :], ALU.add).then_inc(sq_ready, 1)
            for c in range(2, RING):
                split(c, c)
            inverse_rms(0)
            take_rstd(0)
            dve.wait_ge(ones_ready, 2)

            with dve.Fori(0, KC // RING) as i:
                steps.enter(i, 3 * RING)
                for n in range(RING):
                    j = i * RING + n
                    tap = [cst[:, bass.ds(j + (TAPS + k * KC), 1)] for k in range(3)]
                    for part in range(3):
                        c = 3 * n + part
                        p = i * 3 * RING + (IN0 + c)
                        dve.wait_ge(panel_done, p + (1 + CREDIT))
                        bank = banks[c % RING][:, :]
                        if part == 0:
                            dve.tensor_tensor(gate[:, :], bank, rstd2[:, :], ALU.mult).then_inc(bank_free, 1)
                            dve.wait_ge(bank_free, p + (1 + CREDIT))
                        elif part == 1:
                            dve.tensor_tensor(cu[:, 2:], gate[:, :], bank, ALU.mult).then_inc(bank_free, 1)
                            dve.wait_ge(bank_free, p + (1 + CREDIT))
                            dve.tensor_scalar(conv[:, 0, :], cu[:, 2:], tap[0], None,
                                              ALU.mult).then_inc(dve_step, steps.add())
                            for k in (1, 2):
                                dve.wait_ge(dve_step, steps.count())
                                dve.scalar_tensor_tensor(out=conv[:, k, :], in0=cu[:, 2 - k:2 - k + SEQ],
                                                         scalar=tap[k], in1=conv[:, k - 1, :], op0=ALU.mult,
                                                         op1=ALU.add).then_inc(dve_step, steps.add())
                        else:
                            dve.tensor_tensor(gate[:, :], bank, rstd[:, :], ALU.mult).then_inc(bank_free, 1)
                            dve.wait_ge(bank_free, p + (1 + CREDIT))
                            dve.wait_ge(dve_step, steps.count())
                            dve.tensor_tensor(mixed[:, :], conv[:, 2, :], gate[:, :], ALU.mult).then_inc(mixed_ready, 1)
                            dve.wait_ge(zhi_done, j + 1)
                            lo_part(z_lo[:, j, :], mixed[:, :], z_hi[:, j, :], z_ready)
                        ahead(IN0, i, c, 3)
                steps.leave(KC // RING)
            with dve.Fori(0, KC // RING) as i:
                for c in range(RING):
                    j = i * RING + c
                    dve.wait_ge(panel_done, j + (OUT0 + 1 + CREDIT))
                    dve.tensor_tensor(h[:, j, :], h[:, j, :], banks[c][:, :], ALU.add).then_inc(bank_free, 1)
                    normed(xn_hi, xn_lo, GMLP0, j, xhi_done, j + (X_MLP0 + 1), xn_ready)
                    ahead(OUT0, i, c)
            mlp(MLP0, Z_MLP0, 1, ((xn_hi, xn_lo, MIX1, xhi_done, X_MIX1, xn_ready),
                                  (xkv_hi, xkv_lo, GKV, kvhi_done, 0, xkv_ready)))

            def copy_v(i, g):
                dve.wait_ge(ob_filled, i * 9 + (g + 1))
                v = v_sb[:, g, :, :].rearrange("p t (a c) -> p t a c", c=HEAD)[:, :, 0:3:2, :]
                dve.tensor_copy(v, banks[O_BANK][:, :].rearrange("p (t a c) -> p t a c", t=TILES,
                                                                 a=2)).then_inc(ob_free, 1)

            def combine(i, unit):
                g, e, _ = UNITS[unit]
                dve.wait_ge(ob_filled, i * 9 + (4 + unit))
                if g == 0:
                    dve.tensor_copy(acc[:, e, :], banks[O_BANK][:, :]).then_inc(ob_free, 1)
                else:
                    dve.wait_ge(ob_free, i * 9 + (3 + unit))
                    total = order(acc[:, e, :], g)
                    dve.tensor_tensor(total, total, grouped(banks[O_BANK][:, :], g), ALU.add).then_inc(ob_free, 1)

            def normalize(i):
                dve.wait_ge(ob_free, i * 9 + 10)
                low, high = slice(0, HEAD), slice(HEAD, P)
                dve.tensor_copy(rec[low, :], acc[high, 0, :]).then_inc(dve_step, steps.add())
                dve.tensor_copy(rec[high, :], acc[low, 1, :]).then_inc(dve_step, steps.add())
                dve.wait_ge(dve_step, steps.count())
                dve.reciprocal(rec[:, :], rec[:, :]).then_inc(dve_step, steps.add())
                dve.wait_ge(dve_step, steps.count())
                dve.tensor_tensor(o_t[low, i, :], acc[low, 0, :], rec[low, :], ALU.mult).then_inc(dve_step, steps.add())
                dve.tensor_tensor(o_t[high, i, :], acc[high, 1, :], rec[high, :], ALU.mult).then_inc(ot_ready, 1)

            def score_pieces(i, g):
                def maxima(n, e, c0, tiles):
                    dve.wait_ge(s_used, i * N_PIECES + (n + 3))
                    if g == 0 and n % 2 == 0:
                        runs = [(0, 1, 1), (1, 1, 2)]
                    else:
                        runs = [(tiles[0][0], len(tiles), tiles[0][2])]
                    for t, nt, nk in runs:
                        m0 = (g * TILES + t) * 2 + e
                        s = sc[:, e, c0:c0 + nt * nk * P].rearrange("p (t k) -> p t k", t=nt)
                        ins = dve.tensor_reduce(mx[:, m0:m0 + 2 * (nt - 1) + 1:2], s, AX.X, ALU.max)
                        c0 += nt * nk * P
                    return ins
                before = None
                for n, (e, c0, tiles) in enumerate(PIECES[g]):
                    n += PIECE0[g]
                    width = sum(nk for _, _, nk in tiles) * P
                    dve.wait_ge(s_done, i * N_PIECES + (n + 1))
                    bank = banks[S_BANK + n % 2][:, 0:width]
                    out = sc[:, e, c0:c0 + width]
                    if g == 0:
                        far = dst[:, (0 if n % 2 == 0 else P):][:, 0:width]
                    else:
                        far = dst[:, (4 + g) * P:(5 + g) * P].unsqueeze(1).broadcast_to([P, TILES, P])
                        bank, out = (a.rearrange("p (t k) -> p t k", t=TILES) for a in (bank, out))
                    dve.scalar_tensor_tensor(out=out, in0=far, scalar=slope_now[:, e:e + 1], in1=bank,
                                             op0=ALU.mult, op1=ALU.add).then_inc(s_used, 1)
                    if before:
                        maxima(*before)
                    before = (n, e, c0, tiles)
                maxima(*before).then_inc(mx_ready, 1)

            def join_rows(i, g):
                n = ROWS_PIECE[g]
                dve.wait_ge(s_done, i * N_PIECES + (n + 1))
                row = banks[S_BANK + n % 2][0:2, :]
                joint = order(rows[0:2, 0, :], g)
                if g == 0:
                    dve.tensor_copy(joint, row).then_inc(s_used, 1)
                else:
                    dve.wait_ge(s_used, i * N_PIECES + (ROWS_PIECE[g - 1] + 3))
                    if g == 2:
                        dve.tensor_tensor(grouped(rows[0:2, 1, :], g), joint, grouped(row, g), ALU.max)
                    dve.tensor_tensor(joint, joint, grouped(row, g), ALU.max).then_inc(s_used, 1)

            def negate_maxima(i):
                n = BACK_PIECE
                dve.wait_ge(s_done, i * N_PIECES + (n + 1))
                dve.tensor_scalar(negm[:, :], banks[S_BANK + n % 2][:, 0:MAXES], -1.0, None, ALU.mult).then_inc(s_used, 1)

            def pair(i, first):
                dve.tensor_copy(slope_now[:, :], cst[:, bass.ds(i * 2 + SLOPES, 2)]).then_inc(dve_step, steps.add())
                dve.wait_ge(dve_step, steps.count())
                for q in range(PER_PAIR):
                    p = i * PER_PAIR + (ATT0 + q)
                    dve.wait_ge(panel_done, p + (1 + CREDIT))
                    g = q // 2 if q < 6 else q - 6
                    to = (k_t, q_t)[q % 2][:, g, :] if q < 6 else v_t[:, g % 2, :]
                    bank = order(banks[q % RING_ATT][:, :], g)
                    if q in (1, 3, 5):
                        dve.scalar_tensor_tensor(out=grouped(to, g), in0=bank, scalar=HEAD ** -0.5,
                                                 in1=order(rstd[:, :], g), op0=ALU.mult,
                                                 op1=ALU.mult).then_inc(bank_free, 1)
                    else:
                        dve.tensor_tensor(grouped(to, g), bank, order(rstd[:, :], g), ALU.mult).then_inc(bank_free, 1)
                    for before, what, n in AFTER[q]:
                        if before and first:
                            continue
                        j = i - 1 if before else i
                        if what == "scores":
                            score_pieces(j, n)
                        elif what == "rows":
                            join_rows(j, n)
                        elif what == "back":
                            negate_maxima(j)
                        elif what == "turn_v":
                            copy_v(j, n)
                        elif what == "attend":
                            combine(j, n)
                    split(p + RING_ATT, q % RING_ATT)
                if not first:
                    normalize(i - 1)

            inverse_rms(2)
            take_rstd(2)
            dve.wait_ge(dst_ready, 16)
            pair(0, True)
            with dve.Fori(1, PAIRS) as i:
                steps.enter(i - 1, 5)
                pair(i, False)
                steps.leave(PAIRS - 1)
            last = PAIRS - 1
            copy_v(last, 2)
            dve.wait_ge(ohi_done, 1)
            lo_part(o_lo[:, 0:last, :], o_t[:, 0:last, :], o_hi[:, 0:last, :], o_ready)
            for unit in range(3):
                combine(last, unit)
            split(MLP1 - 1, RING - 1)
            for unit in range(3, 6):
                combine(last, unit)
            normalize(last)
            dve.wait_ge(ohi_done, 2)
            lo_part(o_lo[:, last, :], o_t[:, last, :], o_hi[:, last, :], o_ready)
            dve.sem_inc(bank_free, KC // 2)
            for j in range(KC + 1):
                if j < KC:
                    dve.wait_ge(panel_done, WO0 + j // 2 + 1 + CREDIT)
                    dve.tensor_tensor(h[:, j, :], h[:, j, :], banks[j][:, :], ALU.add).then_inc(h_ready, 1)
                if j:
                    dve.wait_ge(h_ready, KC + j)
                    normed(xn_hi, xn_lo, GMLP1, j - 1, xhi_done, X_MLP1 + j, xn_ready)
                    if j % 2 == 0:
                        ahead(WO0, 0, j // 2 - 1)
            mlp(MLP1, Z_MLP1, 3, ())

            inverse_rms(4)
            take_rstd(4)
            for k in range(KC):
                dve.scalar_tensor_tensor(out=final[:, k, :], in0=h[:, k, :], scalar=cst[:, GFIN + k:GFIN + k + 1],
                                         in1=rstd[:, :], op0=ALU.mult, op1=ALU.mult).then_inc(out_ready, 1)

        @block.gpsimd
        def _(pool):
            pool.memset(ones[:, :], 1.0).then_inc(ones_ready, 1)
            pool.memset(cu[:, 0:2], 0.0).then_inc(ones_ready, 1)
            steps = Steps()

            def squares(n, chunk_ready, chunks=KC, done=sq_ready):
                if n:
                    pool.wait_ge(ss_done, n)
                for k in range(chunks):
                    pool.wait_ge(*chunk_ready(k))
                    if steps.count():
                        pool.wait_ge(sq_step, steps.count())
                    to = sq if k else sq_sum
                    pool.tensor_tensor(to[:, :], h[:, k, :], h[:, k, :], ALU.mult).then_inc(sq_step, steps.add())
                    if k:
                        pool.wait_ge(sq_step, steps.count())
                        ins = pool.tensor_tensor(sq_sum[:, :], sq_sum[:, :], sq[:, :], ALU.add)
                        if k < chunks - 1:
                            ins.then_inc(sq_step, steps.add())
                        else:
                            ins.then_inc(done, 1)

            squares(0, lambda k: (x_ready[k], 16), KC // 2, x_squares)
            squares(1, lambda k: (bank_free, OUT0 + k + 1 + CREDIT))
            squares(2, lambda k: (h_ready, k + 1), KC - 1)
            pool.wait_ge(panel_done, ATT0 + CREDIT)
            pool.memset(v_sb[:, :, :, HEAD:2 * HEAD], 1.0).then_inc(vones_ready, 1)
            squares(3, lambda k: (h_ready, KC + k + 1))
            squares(4, lambda k: (h_ready, 2 * KC + k + 1), KC - 1)


def build(nc, arrays):
    ins = {n: nc.dram_tensor(n, a.shape, F32, kind="ExternalInput").ap() for n, a in arrays.items()}
    out_t = nc.dram_tensor("out_t", (KC, P, SEQ), F32, kind="ExternalOutput").ap()
    yoco_trunk(nc, ins["x_t"], ins["weights"], ins["consts"], ins["dist"], ins["ident"], out_t)


def kernel(x, norm_mix, norm_mlp, w_a_in, conv_w, w_a_out, norm_kv, w_kv, w_q, w_o, w_up, w_down, norm_final):
    import numpy as np
    import concourse.bacc as bacc
    from concourse.bass_utils import run_bass_kernel_spmd

    f = np.float32
    x, norm_mix, norm_mlp, w_a_in, conv_w, w_a_out, norm_kv, w_kv, w_q, w_o, w_up, w_down, norm_final = (
        np.asarray(a) for a in (x, norm_mix, norm_mlp, w_a_in, conv_w, w_a_out, norm_kv, w_kv, w_q, w_o,
                                w_up, w_down, norm_final))

    def blocks(w, row, col, rows=D):
        return w[row:row + rows, col:col + P].reshape(rows // P, P, P).transpose(1, 0, 2)

    panels = []
    for j in range(KC):
        panels += [blocks(w_a_in[0], 0, part * D + j * P) for part in (1, 2, 0)]
    panels += [blocks(w_a_out[0], 0, j * P) for j in range(KC)]

    def mlp(layer):
        for half in range(2):
            for j in range(ZC):
                yield blocks(w_up[layer], 0, half * HALF + j * P)
            for j in range(KC):
                for part in range(2):
                    yield blocks(w_down[layer], half * HALF + part * D, j * P)

    panels += mlp(0)
    width = H_G * HEAD
    for pair in range(PAIRS):
        for g in range(N_GROUPS):
            panels += [blocks(w_kv, 0, g * 2 * width + pair * P), blocks(w_q[0], 0, g * width + pair * P)]
        panels += [blocks(w_kv, 0, (g * 2 + 1) * width + pair * P) for g in range(N_GROUPS)]
    for j in range(0, KC, 2):
        panels.append(np.concatenate([blocks(w_o[0], 0, (j + s) * P, width) for s in range(2)], axis=1))
    panels += mlp(1)

    consts = np.zeros((P, N_CONST), f)
    gains = (norm_mix[0], norm_mlp[0], norm_kv, norm_mix[1], norm_mlp[1], norm_final)
    for n, gain in enumerate(gains + tuple(conv_w[0])):
        consts[:, n * KC:(n + 1) * KC] = gain.reshape(KC, P).T
    consts[:, SLOPES:SLOPES + H_G] = [-(2.0 ** -(n + 1)) for n in range(H_G)]
    consts[:, EPSC] = EPS

    a, c = np.arange(P)[:, None], np.arange(P)[None, :]
    own = np.where(c <= a, a - c, MASKED).astype(f)
    prev = np.where(c >= a, P + a - c, MASKED).astype(f)
    n2 = SEQ // DILATIONS[2]
    dist = np.concatenate([own, prev, own, prev, own, np.where(c <= a, DILATIONS[1] * (a - c), MASKED),
                           np.where((c <= a) & (a // n2 == c // n2),
                                    DILATIONS[2] * (a - c), MASKED)], axis=1).astype(f)

    arrays = {
        "x_t": np.ascontiguousarray(x[0].T.reshape(KC, P, SEQ)),
        "weights": np.stack([p.reshape(P, PANEL) for p in panels]),
        "consts": consts, "dist": dist, "ident": np.eye(P, dtype=f),
    }
    nc = bacc.Bacc("TRN2", target_bir_lowering=False, num_devices=1)
    build(nc, arrays)
    r = run_bass_kernel_spmd(nc, [arrays], core_ids=[0])
    return r.results[0]["out_t"].reshape(D, SEQ).T[None]
```

```python
from contextlib import ExitStack

import concourse.bass as bass
from concourse import mybir

F32 = mybir.dt.float32
F32R = mybir.dt.float32r
ALU = mybir.AluOpType
ACT = mybir.ActivationFunctionType
AX = mybir.AxisListType

P = 128
SEQ = 512
D = 1024
KC = D // P
FF = 4 * D
HALF = FF // 2
ZC = HALF // P
N_GROUPS, H_G, HEAD = 3, 8, 64
PAIRS = H_G // 2
DILATIONS = (1, 4, 16)
STRIDES = (1, 4, 4)
TILES = SEQ // P
EPS = 1e-5
MASKED = 2.0 ** 126

PANEL = KC * P
RING = 4
RING_ATT = 3
CREDIT = RING
PER_PAIR = 3 * N_GROUPS

IN0 = 0
OUT0 = IN0 + 3 * KC
MLP0 = OUT0 + KC
HALF_PANELS = ZC + 2 * KC
ATT0 = MLP0 + 2 * HALF_PANELS
WO0 = ATT0 + PAIRS * PER_PAIR
MLP1 = WO0 + KC // 2
N_PANELS = MLP1 + 2 * HALF_PANELS
assert IN0 % RING == OUT0 % RING == MLP0 % RING == ATT0 % RING == WO0 % RING == MLP1 % RING == 0

MIX0, GMLP0, GKV, MIX1, GMLP1, GFIN = (n * KC for n in range(6))
TAPS = 6 * KC
SLOPES = TAPS + 3 * KC
EPSC = SLOPES + H_G
N_CONST = EPSC + 1

SC0, SC1, SC2 = 0, 7 * P, 11 * P
SCORES = 15 * P
SC = (SC0, SC1, SC2)
TILE_COLS = ((0, P), (P, 3 * P), (3 * P, 5 * P), (5 * P, 7 * P))
SETS = (
    (0, SC0, ((0, 0, 1), (1, 0, 2))),
    (0, SC0 + 3 * P, ((2, 1, 2), (3, 2, 2))),
    (1, SC1, tuple((t, t, 1) for t in range(TILES))),
    (2, SC2, tuple((t, t, 1) for t in range(TILES))),
)
PIECE0, ROWS_PIECE, BACK_PIECE, N_PIECES = (0, 2, 5, 7), (4, 9), (10, 11), 12
LOTS = ((0, 0, 0, 4), (0, 0, 4, 3), (0, 1, 0, 4), (0, 1, 4, 3), (1, 0, 0, 4), (2, 0, 0, 4), (1, 1, 0, 4), (2, 1, 0, 4))
UNITS = ((0, 0, (0, 1)), (0, 1, (2, 3)), (1, 0, (4, 5)), (1, 1, (6, 7)))
O_USES = N_GROUPS + len(UNITS)
AFTER = (
    ((True, "turn_v", 2), (True, "turn_p", 0), (True, "turn_p", 1)),
    ((True, "turn_p", 2), (True, "turn_p", 3), (True, "attend", 0)),
    ((True, "attend", 1), (False, "scores", 0)),
    ((True, "turn_p", 4), (True, "turn_p", 5), (False, "scores", 1)),
    ((False, "rows", 0), (True, "attend", 2), (True, "turn_p", 6), (True, "turn_p", 7)),
    ((True, "attend", 3), (False, "scores", 2)),
    ((False, "scores", 3),),
    ((False, "rows", 1), (False, "turn_v", 0)),
    ((False, "turn_v", 1),),
)
FINAL_DVE, FINAL_POOL = (0, 1, 3, 6, 7), (2, 4, 5)
MAXES, JOINT = N_GROUPS * TILES * 2, 2 * TILES * 2


class Steps:

    def __init__(self):
        self.before, self.here, self.turn, self.per = 0, 0, 0, 0

    def add(self):
        self.here += 1
        return 1

    def count(self):
        return self.turn * self.per + (self.before + self.here) if self.per else self.before + self.here

    def enter(self, turn, per):
        self.before, self.here, self.turn, self.per = self.before + self.here, 0, turn, per

    def leave(self, turns):
        assert self.here == self.per, (self.here, self.per)
        self.before, self.here, self.turn, self.per = self.before + turns * self.per, 0, 0, 0


def yoco_trunk(nc, x_t, weights, consts, dist, ident, out_t):
    ctx = ExitStack()
    with ctx:
        base = (nc.sbuf_base + 63) // 64 * 64
        slab = ctx.enter_context(nc.sbuf_tensor("slab", [P, (nc.sbuf_usable_end - base - 128) // 4], F32))
        at = [base]
        end = nc.sbuf_usable_end - 64

        def place(name, shape, dt, offset=None):
            size = 4
            for n in shape:
                size *= n
            where = at[0] if offset is None else offset
            if offset is None:
                at[0] += (size + 31) // 32 * 32
                assert at[0] <= end, (name, at[0] - end)
            t = nc.alloc_sbuf_tensor_at(name, [P, *shape], dtype=dt, offset=where)
            return t, where + (size + 31) // 32 * 32

        h, _ = place("h", [KC, SEQ], F32)
        xn_hi, _ = place("xn_hi", [KC, SEQ], F32R)
        xn_lo, _ = place("xn_lo", [KC, SEQ], F32R)
        kv_area = at[0]
        xkv_hi, _ = place("xkv_hi", [KC, SEQ], F32R)
        xkv_lo, _ = place("xkv_lo", [KC, SEQ], F32R)
        z_area = at[0]
        z_hi, _ = place("z_hi", [ZC, SEQ], F32R)
        z_lo, z_end = place("z_lo", [ZC, SEQ], F32R)
        w_raw, _ = place("w_raw", [RING, PANEL], F32)
        hi_area = at[0]
        w_hi, _ = place("w_hi", [RING, PANEL], F32R)
        lo_area = at[0]
        w_lo, _ = place("w_lo", [RING, PANEL], F32R)
        rstd, _ = place("rstd", [SEQ], F32)
        rstd2, _ = place("rstd2", [SEQ], F32)
        sq_area = at[0]
        sq_sum, _ = place("sq_sum", [SEQ], F32)
        sq, _ = place("sq", [SEQ], F32)
        tmp, _ = place("tmp", [2, SEQ], F32)
        tmp2, _ = place("tmp2", [SEQ], F32)
        cst, _ = place("cst", [N_CONST], F32)
        ones, _ = place("ones", [P], F32)
        idn, _ = place("idn", [P], F32)
        ms4, _ = place("ms4", [TILES], F32)
        root4, _ = place("root4", [TILES], F32)
        cu, nxt = place("cu", [SEQ + 2], F32, kv_area)
        conv, nxt = place("conv", [3, SEQ], F32, nxt)
        gate, nxt = place("gate", [SEQ], F32, nxt)
        mixed, nxt = place("mixed", [SEQ], F32, nxt)
        final, _ = place("final", [KC, SEQ], F32, kv_area)
        v_t, _ = place("v_t", [2, SEQ], F32, hi_area + RING_ATT * PANEL * 4)
        dst, _ = place("dst", [7 * P], F32, lo_area + RING_ATT * PANEL * 4)
        k_t, nxt = place("k_t", [N_GROUPS, SEQ], F32, z_area)
        q_t, nxt = place("q_t", [N_GROUPS, SEQ], F32, nxt)
        sc, nxt = place("sc", [2, SCORES], F32, nxt)
        p_t, nxt = place("p_t", [4, SEQ], F32, nxt)
        v_sb, nxt = place("v_sb", [N_GROUPS, TILES, 3 * HEAD], F32, nxt)
        o_t, nxt = place("o_t", [SEQ], F32, nxt)
        o_hi, nxt = place("o_hi", [PAIRS, SEQ], F32R, nxt)
        o_lo, nxt = place("o_lo", [PAIRS, SEQ], F32R, nxt)
        mx, nxt = place("mx", [MAXES], F32, nxt)
        negm, nxt = place("negm", [JOINT], F32, nxt)
        slope_now, nxt = place("slope_now", [2], F32, nxt)
        assert nxt <= z_end, nxt - z_end
        rows, nxt = place("rows", [SEQ], F32, sq_area)
        rec, _ = place("rec", [SEQ], F32, nxt)
        acc = tmp

        banks = [ctx.enter_context(nc.psum_tensor(f"bank{n}", [P, SEQ], F32)) for n in range(8)]
        STAT = O_BANK = 7
        S_BANK, T_BANK = 3, 5

        def sem(name):
            return ctx.enter_context(nc.semaphore(name))

        raw_ready = [sem(f"raw_ready{n}") for n in range(RING)]
        x_ready = [sem(f"x_ready{n}") for n in range(KC)]
        half_ready, half_hi, half_lo = sem("half_ready"), sem("half_hi"), sem("half_lo")
        cst_ready, idn_ready, dst_ready = sem("cst_ready"), sem("idn_ready"), sem("dst_ready")
        ones_ready = sem("ones_ready")
        vones_ready = sem("vones_ready")
        hi_done = sem("hi_done")
        lo_done = sem("lo_done")
        panel_done = sem("panel_done")
        bank_free = sem("bank_free")
        xhi_done = sem("xhi_done")
        kvhi_done = sem("kvhi_done")
        zhi_done = sem("zhi_done")
        ohi_done = sem("ohi_done")
        xn_ready, xkv_ready = sem("xn_ready"), sem("xkv_ready")
        z_ready, o_ready = sem("z_ready"), sem("o_ready")
        r_done = sem("r_done")
        mixed_ready = sem("mixed_ready")
        h_ready = sem("h_ready")
        sq_step = sem("sq_step")
        sq_ready = sem("sq_ready")
        ss_done = sem("ss_done")
        std_done = sem("std_done")
        inv_ready = sem("inv_ready")
        inv_spread = sem("inv_spread")
        x_squares = sem("x_squares")
        last_square = sem("last_square")
        dve_step = sem("dve_step")
        s_done, s_used = sem("s_done"), sem("s_used")
        mx_ready = sem("mx_ready")
        p_ready = sem("p_ready")
        t_done, t_used = sem("t_done"), sem("t_used")
        ob_filled, ob_free = sem("ob_filled"), sem("ob_free")
        ot_ready = sem("ot_ready")
        out_ready, pool_out_ready = sem("out_ready"), sem("pool_out_ready")
        out_done = sem("out_done")
        rstd_copied = sem("rstd_copied")
        gained = sem("gained")
        wo_done = sem("wo_done")

        X_IN, X_MLP0, X_MIX1, X_MLP1 = 0, KC, 2 * KC, 3 * KC
        Z_Y, Z_MLP0, Z_MLP1 = 0, KC, KC + 2 * ZC

        def order(ap, group):
            r = STRIDES[group]
            return ap if r == 1 else ap.rearrange("p (i r) -> p r i", r=r)

        def grouped(ap, group):
            r = STRIDES[group]
            return ap if r == 1 else ap.rearrange("p (r i) -> p r i", r=r)

        def landed(phase, slot):
            fills = min(phase, ATT0) // RING
            if phase > ATT0:
                fills += (PAIRS * PER_PAIR // RING_ATT if slot < RING_ATT else 0) + (phase - WO0) // RING
            return fills

        block = ctx.enter_context(nc.Block())

        @block.sync
        def _(sp):
            def load(p, slot, ring=RING):
                sp.wait_ge(lo_done, p + (1 - ring + CREDIT))
                sp.dma_start(w_raw[:, slot, :], weights[p]).then_inc(raw_ready[slot], 16)

            sp.dma_start(w_raw[:, 0, 0:PANEL // 2], weights[0][:, 0:PANEL // 2]).then_inc(half_ready, 16)
            sp.dma_start(cst[:, :], consts).then_inc(cst_ready, 16)
            sp.dma_start(h[:, 0, :], x_t[0]).then_inc(x_ready[0], 16)
            sp.dma_start(w_raw[:, 0, PANEL // 2:], weights[0][:, PANEL // 2:]).then_inc(raw_ready[0], 16)
            for k in range(1, KC):
                sp.dma_start(h[:, k, :], x_t[k]).then_inc(x_ready[k], 16)
            for p in range(1, RING):
                load(p, p)
            sp.dma_start(idn[:, :], ident).then_inc(idn_ready, 16)
            with sp.Fori(1, ATT0 // RING) as i:
                for c in range(RING):
                    load(i * RING + c, c)
            for q in range(RING_ATT):
                load(ATT0 + q, q, RING_ATT)
            sp.wait_ge(panel_done, ATT0 + CREDIT)
            sp.dma_start(dst[:, :], dist).then_inc(dst_ready, 16)
            with sp.Fori(0, PAIRS) as i:
                for q in range(PER_PAIR):
                    load(i * PER_PAIR + (ATT0 + RING_ATT + q), q % RING_ATT, RING_ATT)
            load(MLP1 - 1, RING - 1)
            with sp.Fori(MLP1 // RING, N_PANELS // RING) as i:
                for c in range(RING):
                    load(i * RING + c, c)
            for n, k in enumerate(FINAL_DVE):
                sp.wait_ge(out_ready, n + 1)
                sp.dma_start(out_t[k], final[:, k, :]).then_inc(out_done, 16)
                if n % 2 or n == len(FINAL_DVE) - 1:
                    sp.wait_ge(pool_out_ready, n // 2 + 1)
                    k = FINAL_POOL[n // 2]
                    sp.dma_start(out_t[k], final[:, k, :]).then_inc(out_done, 16)
            sp.wait_ge(out_done, 16 * KC)

        @block.tensor
        def _(pe):
            pe.sem_inc(panel_done, CREDIT)

            def products(out, slot, col, hi, lo, chunks, first, last, ready=None):
                for n, k in enumerate(chunks):
                    if ready is not None:
                        pe.wait_ge(ready[0], ready[1] + k + 1)
                    w = slice(col + n * P, col + (n + 1) * P)
                    pe.matmul(out, w_hi[:, slot, w], hi[:, k, :], start=first and n == 0, stop=False)
                    pe.matmul(out, w_hi[:, slot, w], lo[:, k, :], start=False, stop=False)
                    mm = pe.matmul(out, w_lo[:, slot, w], hi[:, k, :], start=False,
                                   stop=last and n == len(chunks) - 1)
                return mm

            def panel(p, slot, bank, hi, lo, chunks=range(KC), first=True, last=True, ready=None, ring=RING,
                      between=None):
                pe.wait_ge(lo_done, p + (1 + CREDIT))
                if first:
                    pe.wait_ge(bank_free, p + (1 - ring + CREDIT))
                out, col = banks[bank][:, :], 0
                if between is not None:
                    col = len(chunks) // 2 * P
                    products(out, slot, 0, hi, lo, chunks[:len(chunks) // 2], first, False, ready)
                    between()
                    chunks, first = chunks[len(chunks) // 2:], False
                products(out, slot, col, hi, lo, chunks, first, last, ready).then_inc(panel_done, 1)

            def stats(n, apart=0):
                for part in range(-1, apart):
                    if part < 0:
                        pe.wait_ge(sq_ready, n + 1)
                    else:
                        pe.wait_ge(last_square, part + 1)
                    for t in range(TILES):
                        squares = (sq_sum if part < 0 else tmp[:, part, :])[:, t * P:(t + 1) * P]
                        mm = pe.matmul(banks[STAT][:, t:t + 1], squares, ones[:, 0:1], start=part < 0 and t == 0,
                                       stop=part == apart - 1 and t == TILES - 1, skip_group_check=True)
                mm.then_inc(ss_done, 1)

            def spread(n):
                pe.wait_ge(inv_ready, n + 1)
                for t in range(TILES):
                    mm = pe.matmul(banks[STAT][:, t * P:(t + 1) * P], root4[:, t:t + 1].broadcast_to([P, P]),
                                   idn[:, :], start=True, stop=True)
                mm.then_inc(inv_spread, 1)

            def mlp(p0, x_count, z_count, norm):
                for half in range(2):
                    up, down = p0 + half * HALF_PANELS, p0 + half * HALF_PANELS + ZC
                    rounds = ZC // RING
                    with pe.Fori(0, rounds - (half == 0)) as i:
                        for c in range(RING):
                            panel(i * RING + (up + c), c, c, xn_hi, xn_lo,
                                  ready=(xn_ready, x_count) if c == 0 else None)
                    if half == 0:
                        stats(norm)
                        for c in range(RING):
                            panel(up + (rounds - 1) * RING + c, c, c, xn_hi, xn_lo)
                        spread(norm)
                    with pe.Fori(0, 2 * KC // 8) as i:
                        for c in range(8):
                            k0 = KC * (c % 2)
                            panel(i * 8 + (down + c), c % RING, c // 2, z_hi, z_lo, chunks=range(k0, k0 + KC),
                                  first=c % 2 == 0, last=c % 2 == 1,
                                  ready=(z_ready, z_count + half * ZC) if c < 2 else None)

            pe.wait_ge(ones_ready, 1)
            for c in range(RING):
                if c == 0:
                    pe.wait_ge(half_lo, 1)
                    products(banks[0][:, :], 0, 0, xn_hi, xn_lo, range(KC // 2), True, False, (xn_ready, X_IN))
                    pe.wait_ge(lo_done, 1 + CREDIT)
                    products(banks[0][:, :], 0, PANEL // 2, xn_hi, xn_lo, range(KC // 2, KC), False, True,
                             (xn_ready, X_IN)).then_inc(panel_done, 1)
                else:
                    panel(IN0 + c, c, c, xn_hi, xn_lo)
                if c == 1:
                    stats(0)
                if c == 2:
                    pe.wait_ge(idn_ready, 16)
                    spread(0)
            with pe.Fori(1, 3 * KC // RING) as i:
                for c in range(RING):
                    panel(i * RING + (IN0 + c), c, c, xn_hi, xn_lo)
            with pe.Fori(0, KC // RING) as i:
                for c in range(RING):
                    panel(i * RING + (OUT0 + c), c, c, z_hi, z_lo, ready=(z_ready, Z_Y) if c == 0 else None)
            mlp(MLP0, X_MLP0, Z_MLP0, 1)

            def scores(i, k):
                g, _, tiles = SETS[k]
                pe.wait_ge(bank_free, i * PER_PAIR + (ATT0 + 2 * g + 2 + CREDIT))
                pe.wait_ge(s_used, i * N_PIECES + (PIECE0[k] + 2))
                col = 0
                for tile, key, nk in tiles:
                    for e in range(2):
                        heads = slice(HEAD * e, HEAD * e + HEAD)
                        mm = pe.matmul(banks[S_BANK + (PIECE0[k] + e) % 2][:, col:col + nk * P],
                                       q_t[heads, g, tile * P:(tile + 1) * P],
                                       k_t[heads, g, key * P:(key + nk) * P], start=True, stop=True)
                        if tile == tiles[-1][0]:
                            mm.then_inc(s_done, 1)
                    col += nk * P

            def turn_maxima(i, k):
                n = ROWS_PIECE[k]
                pe.wait_ge(mx_ready, i * 2 + (k + 1))
                pe.wait_ge(s_used, i * N_PIECES + (n + 1))
                for t in range(TILES):
                    m = (k * TILES + t) * 2
                    mm = pe.transpose(banks[S_BANK + n % 2][0:2, t * P:(t + 1) * P], mx[:, m:m + 2], idn[:, :])
                mm.then_inc(s_done, 1)

            def maxima_back(i, k):
                n = BACK_PIECE[k]
                pe.wait_ge(s_used, i * N_PIECES + (ROWS_PIECE[1] + 3 if k == 0 else n + 1))
                for t in range(TILES):
                    tokens = rows[0:2, t * P:(t + 1) * P] if k == 0 else rows[0:2, t:SEQ:TILES]
                    mm = pe.matmul(banks[S_BANK + n % 2][:, t * 2:t * 2 + 2], tokens, idn[0:2, 0:2],
                                   start=True, stop=True)
                mm.then_inc(s_done, 1)

            def turn_v(i, g):
                pe.wait_ge(bank_free, i * PER_PAIR + (ATT0 + 6 + g + 1 + CREDIT))
                pe.wait_ge(ob_free, i * O_USES + (g + 1))
                for t in range(TILES):
                    mm = pe.transpose(banks[O_BANK][:, t * P:(t + 1) * P], v_t[:, g % 2, t * P:(t + 1) * P],
                                      idn[:, :])
                mm.then_inc(ob_filled, 1)

            def turn_p(i, n):
                g, e, tile, nt = LOTS[n]
                pe.wait_ge(p_ready, i * 2 + (1 if g == 0 else 2))
                pe.wait_ge(t_used, i * 8 + (n + 1))
                for t in range(nt):
                    c = SC[g] + (tile + t) * P
                    mm = pe.transpose(banks[T_BANK + n % 2][:, t * P:(t + 1) * P], sc[:, e, c:c + P], idn[:, :])
                mm.then_inc(t_done, 1)

            def attend(i, unit):
                part, e, lots = UNITS[unit]
                out, vcols = banks[O_BANK], slice(HEAD * e, HEAD * e + P)
                pe.wait_ge(ob_free, i * O_USES + (4 + unit))
                pe.wait_ge(t_used, i * 8 + (lots[-1] + 3))
                if part == 0:
                    for key in range(TILES):
                        n, nq = lots[key // 2], min(2, TILES - key)
                        c = (2 * key - LOTS[n][2]) * P
                        mm = pe.matmul(out[:, key * P:(key + nq) * P], v_sb[:, 0, key, vcols],
                                       p_t[:, n % 4, c:c + nq * P], start=key == 0,
                                       stop=key == TILES - 1, skip_group_check=True)
                else:
                    for t in range(TILES):
                        for n in lots:
                            mm = pe.matmul(out[:, t * P:(t + 1) * P], v_sb[:, LOTS[n][0], t, vcols],
                                           p_t[:, n % 4, t * P:(t + 1) * P], start=n == lots[0],
                                           stop=n == lots[-1])
                mm.then_inc(ob_filled, 1)

            def pair(i, first):
                for q in range(PER_PAIR):
                    hi, lo = (xn_hi, xn_lo) if q in (1, 3, 5) else (xkv_hi, xkv_lo)
                    ready = ((xkv_ready, 0), (xn_ready, X_MIX1))[q] if first and q < 2 else None

                    def back():
                        maxima_back(i, 0)
                        maxima_back(i, 1)

                    between = back if q == PER_PAIR - 1 else (lambda: spread(2)) if first and q == 1 else None
                    panel(i * PER_PAIR + (ATT0 + q), q % RING_ATT, q % RING_ATT, hi, lo, ready=ready,
                          ring=RING_ATT, between=between)
                    if first and q == 0:
                        stats(2)
                    for before, what, n in AFTER[q]:
                        if before and first:
                            continue
                        j = i - 1 if before else i
                        if what == "scores":
                            scores(j, n)
                        elif what == "rows":
                            turn_maxima(j, n)
                        elif what == "turn_v":
                            turn_v(j, n)
                        elif what == "turn_p":
                            turn_p(j, n)
                        else:
                            attend(j, n)

            pair(0, True)
            pe.wait_ge(vones_ready, 1)
            with pe.Fori(1, PAIRS) as i:
                pair(i, False)

            last = PAIRS - 1

            def out_part(j, chunks):
                c, first = (j % 2 * PAIRS + chunks[0]) * P, chunks[0] == 0
                pe.wait_ge(lo_done, WO0 + (j // 2 + 1 + CREDIT))
                return products(banks[j][:, :], j // 2, c, o_hi, o_lo, chunks, first, chunks[-1] == last)

            pe.wait_ge(o_ready, last)
            pe.wait_ge(bank_free, WO0 - 2 + CREDIT)
            out_part(0, range(last))
            turn_v(last, 2)
            out_part(1, range(last))
            turn_p(last, 0)
            turn_p(last, 1)
            turn_p(last, 2)
            turn_p(last, 3)
            attend(last, 0)
            turn_p(last, 4)
            turn_p(last, 5)
            attend(last, 1)
            turn_p(last, 6)
            turn_p(last, 7)
            attend(last, 2)
            out_part(2, range(last))
            attend(last, 3)
            pe.wait_ge(s_used, N_PIECES * PAIRS + 2)
            out_part(3, range(last))
            out_part(4, range(last))
            pe.wait_ge(t_used, 8 * PAIRS + 2)
            out_part(5, range(last))
            out_part(6, range(last))
            pe.wait_ge(o_ready, PAIRS)
            for j in range(KC):
                mm = out_part(j, range(last, PAIRS) if j < KC - 1 else range(PAIRS))
                mm.then_inc(panel_done if j % 2 else wo_done, 1)
            mlp(MLP1, X_MLP1, Z_MLP1, 3)
            stats(4, apart=2)
            spread(4)

        @block.scalar
        def _(act):
            act.sem_inc(t_used, 2)

            def split(p, slot, fills, ring=RING):
                act.wait_ge(raw_ready[slot], fills * 16)
                act.wait_ge(panel_done, p + (1 - ring + CREDIT))
                act.copy(w_hi[:, slot, :], w_raw[:, slot, :]).then_inc(hi_done, 1)

            def ahead(phase, turn, c, rings=1):
                slot = c % RING
                split(turn * (rings * RING) + (phase + c + RING), slot,
                      turn * rings + (landed(phase, slot) + 2 + c // RING))

            def normed(hi, gain, j, done):
                act.activation(hi[:, j, :], h[:, j, :], ACT.Copy, scale=cst[:, bass.ds(j + gain, 1)]).then_inc(done, 1)

            def root(n):
                act.wait_ge(ss_done, n + 1)
                act.activation(root4[:, :], banks[STAT][:, 0:TILES], ACT.Sqrt, scale=1.0 / D,
                               bias=cst[:, EPSC:EPSC + 1]).then_inc(std_done, 1)

            def mlp(p0, z_count, norm, h_count, gains):
                for half in range(2):
                    up, down = p0 + half * HALF_PANELS, p0 + half * HALF_PANELS + ZC
                    relus = half * ZC + (0 if p0 == MLP0 else 2 * ZC)
                    rounds = ZC // RING

                    def up_turn(i):
                        for c in range(RING):
                            p = i * RING + (up + c)
                            act.wait_ge(bank_free, p + (1 - 2 + CREDIT))
                            act.wait_ge(panel_done, p + (1 + CREDIT))
                            act.activation(tmp[:, c % 2, :], banks[c][:, :], ACT.Relu).then_inc(r_done, 1)
                            act.wait_ge(r_done, i * RING + (relus + c + 1))
                            act.activation(z_hi[:, i * RING + c, :], tmp[:, c % 2, :], ACT.Square).then_inc(zhi_done, 1)
                            ahead(up, i, c)

                    with act.Fori(0, rounds - (half == 0)) as i:
                        up_turn(i)
                    if half == 0:
                        root(norm)
                        up_turn(rounds - 1)

                    def down_turn(i, following=True):
                        for c in range(2 * RING):
                            if half == 1 and c % 2 == 1:
                                if gains:
                                    act.wait_ge(h_ready, i * RING + (h_count + c // 2 + 1))
                                    for hi, gain, done in gains:
                                        normed(hi, gain, i * RING + c // 2, done)
                            if following or (c < RING or p0 == MLP0 and c < 2 * RING - 1):
                                ahead(down, i, c, 2)

                    if half == 0:
                        with act.Fori(0, 2) as i:
                            down_turn(i)
                    else:
                        down_turn(0)
                        down_turn(1, following=False)
                        if p0 == MLP1:
                            for k in (KC - 2, KC - 1):
                                act.wait_ge(h_ready, h_count + k + 1)
                                act.activation(tmp[:, k - (KC - 2), :], h[:, k, :],
                                               ACT.Square).then_inc(last_square, 1)

            act.wait_ge(ones_ready, 1)
            act.copy(root4[:, 0:1], ones[:, 0:1])
            act.wait_ge(half_ready, 16)
            act.copy(w_hi[:, 0, 0:PANEL // 2], w_raw[:, 0, 0:PANEL // 2]).then_inc(half_hi, 1)
            act.wait_ge(cst_ready, 16)
            for k in range(KC):
                act.wait_ge(x_ready[k], 16)
                normed(xn_hi, MIX0, k, xhi_done)
                if k == 0:
                    act.wait_ge(raw_ready[0], 16)
                    act.copy(w_hi[:, 0, PANEL // 2:], w_raw[:, 0, PANEL // 2:]).then_inc(hi_done, 1)
            for c in range(1, RING):
                split(c, c, 1)
            root(0)
            with act.Fori(0, KC // RING) as i:
                for c in range(3 * RING):
                    if c % 3 == 2:
                        act.wait_ge(mixed_ready, i * RING + (c // 3 + 1))
                        act.copy(z_hi[:, i * RING + c // 3, :], mixed[:, :]).then_inc(zhi_done, 1)
                    ahead(IN0, i, c, 3)
            with act.Fori(0, KC // RING) as i:
                for c in range(RING):
                    act.wait_ge(bank_free, i * RING + (OUT0 + c + 1 + CREDIT))
                    normed(xn_hi, GMLP0, i * RING + c, xhi_done)
                    ahead(OUT0, i, c)
            mlp(MLP0, Z_MLP0, 1, 0, ((xn_hi, MIX1, xhi_done), (xkv_hi, GKV, kvhi_done)))

            def exps(i, k):
                act.wait_ge(s_used, i * N_PIECES + (BACK_PIECE[k] + 3))
                for e in range(2):
                    for t in range(TILES):
                        if k == 0:
                            s = sc[:, e, slice(*TILE_COLS[t])]
                        else:
                            s = sc[:, e, SC1:].rearrange("p (g t k) -> p t g k", g=2, t=TILES)[:, t, :, :]
                        m = (k * TILES + t) * 2 + e
                        ins = act.activation(s, s, ACT.Exp, bias=negm[:, m:m + 1])
                ins.then_inc(p_ready, 1)

            def copy_lot(i, n):
                nt = LOTS[n][3]
                act.wait_ge(t_done, i * 8 + (n + 1))
                act.wait_ge(ob_filled, i * O_USES + (3 if n < 4 else 4 + (n - 4) // 2))
                act.copy(p_t[:, n % 4, 0:nt * P], banks[T_BANK + n % 2][:, 0:nt * P]).then_inc(t_used, 1)

            def o_hi_part(i):
                act.wait_ge(ot_ready, i + 1)
                act.copy(o_hi[:, i, :], o_t[:, :]).then_inc(ohi_done, 1)

            def pair(i, first):
                for q in range(PER_PAIR):
                    if not first:
                        for _, what, n in AFTER[q]:
                            if what == "turn_p":
                                copy_lot(i - 1, n)
                        if q == 7:
                            o_hi_part(i - 1)
                    if q == 8:
                        exps(i, 0)
                        exps(i, 1)
                    slot = q % RING_ATT
                    split(i * PER_PAIR + (ATT0 + q + RING_ATT), slot,
                          i * (PER_PAIR // RING_ATT) + (landed(ATT0, slot) + q // RING_ATT + 2), RING_ATT)

            root(2)
            pair(0, True)
            with act.Fori(1, PAIRS) as i:
                pair(i, False)
            last = PAIRS - 1
            copy_lot(last, 0)
            copy_lot(last, 1)
            act.wait_ge(ob_filled, last * O_USES + N_GROUPS)
            split(MLP1 - 1, RING - 1, landed(MLP1 - 1, RING - 1) + 1)
            for n in range(2, 8):
                copy_lot(last, n)
            o_hi_part(last)
            for c in range(RING):
                for s in range(2):
                    act.wait_ge(h_ready, KC + 2 * c + s + 1)
                    normed(xn_hi, GMLP1, 2 * c + s, xhi_done)
                if c < 2:
                    ahead(WO0, 0, c)
            for c in (2, 3):
                ahead(WO0, 0, c)
            mlp(MLP1, Z_MLP1, 3, 2 * KC, ())
            root(4)

        @block.vector
        def _(dve):
            dve.sem_inc(lo_done, CREDIT)
            dve.sem_inc(bank_free, CREDIT)
            dve.sem_inc(s_used, 2)
            dve.sem_inc(ob_free, 1)
            steps = Steps()

            def lo_part(lo, x, hi, done):
                dve.tensor_tensor(lo, x, hi.bitcast(F32), ALU.subtract).then_inc(done, 1)

            def split(p, slot):
                dve.wait_ge(hi_done, p + 1)
                lo_part(w_lo[:, slot, :], w_raw[:, slot, :], w_hi[:, slot, :], lo_done)

            def ahead(phase, turn, c, rings=1):
                split(turn * (rings * RING) + (phase + c + RING), c % RING)

            def normed(hi, lo, gain, j, counted, count, done):
                dve.wait_ge(counted, count)
                dve.scalar_tensor_tensor(out=lo[:, j, :], in0=h[:, j, :], scalar=cst[:, bass.ds(j + gain, 1)],
                                         in1=hi[:, j, :].bitcast(F32), op0=ALU.mult,
                                         op1=ALU.subtract).then_inc(done, 1)

            def inverse_rms(n):
                def step(ins):
                    ins.then_inc(dve_step, steps.add())
                    dve.wait_ge(dve_step, steps.count())
                dve.wait_ge(std_done, n + 1)
                dve.tensor_scalar(ms4[:, :], banks[STAT][:, 0:TILES], 1.0 / D, EPS, ALU.mult,
                                  ALU.add).then_inc(dve_step, steps.add())
                step(dve.reciprocal(root4[:, :], root4[:, :]))
                step(dve.tensor_tensor(ms4[:, :], ms4[:, :], root4[:, :], ALU.mult))
                step(dve.tensor_tensor(ms4[:, :], ms4[:, :], root4[:, :], ALU.mult))
                step(dve.tensor_scalar(ms4[:, :], ms4[:, :], -0.5, 1.5, ALU.mult, ALU.add))
                dve.tensor_tensor(root4[:, :], root4[:, :], ms4[:, :], ALU.mult).then_inc(inv_ready, 1)

            def take_rstd(n):
                dve.wait_ge(inv_spread, n + 1)
                dve.tensor_copy(rstd[:, :], banks[STAT][:, :]).then_inc(dve_step, steps.add())
                dve.wait_ge(dve_step, steps.count())
                dve.tensor_tensor(rstd2[:, :], rstd[:, :], rstd[:, :], ALU.mult).then_inc(dve_step, steps.add())
                dve.wait_ge(dve_step, steps.count())

            def mlp(p0, z_count, norm, gains):
                for half in range(2):
                    up, down = p0 + half * HALF_PANELS, p0 + half * HALF_PANELS + ZC
                    relus = half * ZC + (0 if p0 == MLP0 else 2 * ZC)
                    rounds = ZC // RING

                    def up_panel(i, c):
                        dve.wait_ge(z_ready, i * RING + (z_count + half * ZC + c))
                        dve.wait_ge(r_done, i * RING + (relus + c + 1))
                        dve.tensor_tensor(tmp2[:, :], tmp[:, c % 2, :], tmp[:, c % 2, :],
                                          ALU.mult).then_inc(bank_free, 1)
                        dve.wait_ge(bank_free, i * RING + (up + c + 1 + CREDIT))
                        dve.wait_ge(zhi_done, i * RING + (z_count + half * ZC + c + 1))
                        lo_part(z_lo[:, i * RING + c, :], tmp2[:, :], z_hi[:, i * RING + c, :], z_ready)
                        ahead(up, i, c)

                    with dve.Fori(0, rounds - (half == 0)) as i:
                        for c in range(RING):
                            up_panel(i, c)
                    if half == 0:
                        for c in range(RING):
                            up_panel(rounds - 1, c)
                            if c == 0:
                                inverse_rms(norm)
                        take_rstd(norm)
                    dve.wait_ge(z_ready, z_count + (half + 1) * ZC)

                    def down_turn(i, following=True):
                        for c in range(2 * RING):
                            if c % 2 == 1:
                                dve.wait_ge(dve_step, steps.count())
                                j, p = i * RING + c // 2, i * 2 * RING + (down + c)
                                dve.wait_ge(panel_done, p + (1 + CREDIT))
                                dve.tensor_tensor(tmp2[:, :], banks[c // 2][:, :], rstd2[:, :],
                                                  ALU.mult).then_inc(bank_free, 2)
                                dve.wait_ge(bank_free, p + (1 + CREDIT))
                                ins = dve.tensor_tensor(h[:, j, :], h[:, j, :], tmp2[:, :], ALU.add)
                                if half == 0:
                                    ins.then_inc(dve_step, steps.add())
                                else:
                                    ins.then_inc(h_ready, 1)
                                    dve.wait_ge(h_ready, j + ((0 if p0 == MLP0 else 2 * KC) + 1))
                                    for hi, lo, gain, counted, count, done in gains:
                                        normed(hi, lo, gain, j, counted, j + (count + 1), done)
                            if following or (c < RING or p0 == MLP0 and c < 2 * RING - 1):
                                ahead(down, i, c, 2)

                    if half == 0:
                        with dve.Fori(0, 2) as i:
                            steps.enter(i, RING)
                            down_turn(i)
                            steps.leave(2)
                        dve.wait_ge(dve_step, steps.count())
                    else:
                        down_turn(0)
                        down_turn(1, following=False)

            dve.wait_ge(half_hi, 1)
            lo_part(w_lo[:, 0, 0:PANEL // 2], w_raw[:, 0, 0:PANEL // 2], w_hi[:, 0, 0:PANEL // 2], half_lo)
            dve.wait_ge(cst_ready, 16)
            for k in range(KC):
                normed(xn_hi, xn_lo, MIX0, k, xhi_done, X_IN + k + 1, xn_ready)
                if k == 0:
                    dve.wait_ge(hi_done, 1)
                    lo_part(w_lo[:, 0, PANEL // 2:], w_raw[:, 0, PANEL // 2:], w_hi[:, 0, PANEL // 2:], lo_done)
            split(1, 1)
            for k in range(KC // 2, KC):
                first = k == KC // 2
                dve.wait_ge(x_ready[k], 16)
                dve.tensor_tensor(tmp2[:, :] if first else tmp[:, k % 2, :], h[:, k, :], h[:, k, :],
                                  ALU.mult).then_inc(dve_step, steps.add())
                if not first:
                    dve.wait_ge(dve_step, steps.count())
                    dve.tensor_tensor(tmp2[:, :], tmp2[:, :], tmp[:, k % 2, :],
                                      ALU.add).then_inc(dve_step, steps.add())
            dve.wait_ge(dve_step, steps.count())
            dve.wait_ge(x_squares, 1)
            dve.tensor_tensor(sq_sum[:, :], sq_sum[:, :], tmp2[:, :], ALU.add).then_inc(sq_ready, 1)
            for c in range(2, RING):
                split(c, c)
            inverse_rms(0)
            take_rstd(0)
            dve.wait_ge(ones_ready, 2)

            with dve.Fori(0, KC // RING) as i:
                steps.enter(i, 3 * RING)
                for n in range(RING):
                    j = i * RING + n
                    tap = [cst[:, bass.ds(j + (TAPS + k * KC), 1)] for k in range(3)]
                    for part in range(3):
                        c = 3 * n + part
                        p = i * 3 * RING + (IN0 + c)
                        dve.wait_ge(panel_done, p + (1 + CREDIT))
                        bank = banks[c % RING][:, :]
                        if part == 0:
                            dve.tensor_tensor(gate[:, :], bank, rstd2[:, :], ALU.mult).then_inc(bank_free, 1)
                            dve.wait_ge(bank_free, p + (1 + CREDIT))
                        elif part == 1:
                            dve.tensor_tensor(cu[:, 2:], gate[:, :], bank, ALU.mult).then_inc(bank_free, 1)
                            dve.wait_ge(bank_free, p + (1 + CREDIT))
                            dve.tensor_scalar(conv[:, 0, :], cu[:, 2:], tap[0], None,
                                              ALU.mult).then_inc(dve_step, steps.add())
                            for k in (1, 2):
                                dve.wait_ge(dve_step, steps.count())
                                dve.scalar_tensor_tensor(out=conv[:, k, :], in0=cu[:, 2 - k:2 - k + SEQ],
                                                         scalar=tap[k], in1=conv[:, k - 1, :], op0=ALU.mult,
                                                         op1=ALU.add).then_inc(dve_step, steps.add())
                        else:
                            dve.tensor_tensor(gate[:, :], bank, rstd[:, :], ALU.mult).then_inc(bank_free, 1)
                            dve.wait_ge(bank_free, p + (1 + CREDIT))
                            dve.wait_ge(dve_step, steps.count())
                            dve.tensor_tensor(mixed[:, :], conv[:, 2, :], gate[:, :], ALU.mult).then_inc(mixed_ready, 1)
                            dve.wait_ge(zhi_done, j + 1)
                            lo_part(z_lo[:, j, :], mixed[:, :], z_hi[:, j, :], z_ready)
                        ahead(IN0, i, c, 3)
                steps.leave(KC // RING)
            with dve.Fori(0, KC // RING) as i:
                for c in range(RING):
                    j = i * RING + c
                    dve.wait_ge(panel_done, j + (OUT0 + 1 + CREDIT))
                    dve.tensor_tensor(h[:, j, :], h[:, j, :], banks[c][:, :], ALU.add).then_inc(bank_free, 1)
                    normed(xn_hi, xn_lo, GMLP0, j, xhi_done, j + (X_MLP0 + 1), xn_ready)
                    ahead(OUT0, i, c)
            mlp(MLP0, Z_MLP0, 1, ((xn_hi, xn_lo, MIX1, xhi_done, X_MIX1, xn_ready),
                                  (xkv_hi, xkv_lo, GKV, kvhi_done, 0, xkv_ready)))

            def copy_v(i, g):
                dve.wait_ge(ob_filled, i * O_USES + (g + 1))
                v = v_sb[:, g, :, :].rearrange("p t (a c) -> p t a c", c=HEAD)[:, :, 0:3:2, :]
                dve.tensor_copy(v, banks[O_BANK][:, :].rearrange("p (t a c) -> p t a c", t=TILES,
                                                                 a=2)).then_inc(ob_free, 1)

            def combine(i, unit):
                part, e, _ = UNITS[unit]
                dve.wait_ge(ob_filled, i * O_USES + (4 + unit))
                if part == 0:
                    dve.tensor_copy(acc[:, e, :], banks[O_BANK][:, :]).then_inc(ob_free, 1)
                    return
                dve.wait_ge(ob_free, i * O_USES + (3 + unit))
                total = order(acc[:, e, :], 1)
                dve.tensor_tensor(total, total, grouped(banks[O_BANK][:, :], 1), ALU.add).then_inc(ob_free, 1)
                dve.wait_ge(ob_free, i * O_USES + (5 + unit))
                here, there = (slice(0, HEAD), slice(HEAD, P)) if e == 0 else (slice(HEAD, P), slice(0, HEAD))
                dve.tensor_copy(rec[here, :], acc[there, e, :]).then_inc(dve_step, steps.add())

            def invert():
                dve.wait_ge(dve_step, steps.count())
                dve.reciprocal(rec[:, :], rec[:, :]).then_inc(dve_step, steps.add())

            def normalize():
                dve.wait_ge(dve_step, steps.count())
                for e in range(2):
                    half = slice(e * HEAD, (e + 1) * HEAD)
                    ins = dve.tensor_tensor(o_t[half, :], acc[half, e, :], rec[half, :], ALU.mult)
                ins.then_inc(ot_ready, 1)

            def o_lo_part(i):
                dve.wait_ge(ohi_done, i + 1)
                lo_part(o_lo[:, i, :], o_t[:, :], o_hi[:, i, :], o_ready)

            def score_pieces(i, k):
                g, c0, tiles = SETS[k]
                width = sum(nk for _, _, nk in tiles) * P
                for e in range(2):
                    n = PIECE0[k] + e
                    dve.wait_ge(s_done, i * N_PIECES + (n + 1))
                    bank = banks[S_BANK + n % 2][:, 0:width]
                    out = sc[:, e, c0:c0 + width]
                    if g == 0:
                        far = dst[:, (0 if c0 == SC0 else P):][:, 0:width]
                    else:
                        far = dst[:, (4 + g) * P:(5 + g) * P].unsqueeze(1).broadcast_to([P, TILES, P])
                        bank, out = (a.rearrange("p (t k) -> p t k", t=TILES) for a in (bank, out))
                    dve.scalar_tensor_tensor(out=out, in0=far, scalar=slope_now[:, e:e + 1], in1=bank,
                                             op0=ALU.mult, op1=ALU.add).then_inc(s_used, 1)
                runs = [(0, 1, 1), (1, 1, 2)] if k == 0 else [(tiles[0][0], len(tiles), tiles[0][2])]
                for e in range(2):
                    dve.wait_ge(s_used, i * N_PIECES + (PIECE0[k] + e + 3))
                    c = c0
                    for t, nt, nk in runs:
                        m = (g * TILES + t) * 2 + e
                        s = sc[:, e, c:c + nt * nk * P].rearrange("p (t k) -> p t k", t=nt)
                        ins = dve.tensor_reduce(mx[:, m:m + 2 * (nt - 1) + 1:2], s, AX.X, ALU.max)
                        c += nt * nk * P
                if k == 1:
                    ins.then_inc(mx_ready, 1)
                elif k > 1:
                    ins.then_inc(dve_step, steps.add())
                if k == 3:
                    dve.wait_ge(dve_step, steps.count())
                    first, second = (mx[:, n * 2 * TILES:(n + 1) * 2 * TILES] for n in (1, 2))
                    dve.tensor_tensor(first, first, second, ALU.max).then_inc(mx_ready, 1)

            def join_rows(i, k):
                n = ROWS_PIECE[k]
                dve.wait_ge(s_done, i * N_PIECES + (n + 1))
                row = banks[S_BANK + n % 2][0:2, :]
                if k == 0:
                    dve.tensor_copy(rows[0:2, :], row).then_inc(s_used, 1)
                else:
                    dve.wait_ge(s_used, i * N_PIECES + (ROWS_PIECE[0] + 3))
                    joint = order(rows[0:2, :], k)
                    dve.tensor_tensor(joint, joint, grouped(row, k), ALU.max).then_inc(s_used, 1)

            def negate_maxima(i, k):
                n = BACK_PIECE[k]
                dve.wait_ge(s_done, i * N_PIECES + (n + 1))
                m = 2 * TILES
                dve.tensor_scalar(negm[:, k * m:(k + 1) * m], banks[S_BANK + n % 2][:, 0:m], -1.0, None,
                                  ALU.mult).then_inc(s_used, 1)

            def pair(i, first):
                dve.tensor_copy(slope_now[:, :], cst[:, bass.ds(i * 2 + SLOPES, 2)]).then_inc(dve_step, steps.add())
                dve.wait_ge(dve_step, steps.count())
                for q in range(PER_PAIR):
                    p = i * PER_PAIR + (ATT0 + q)
                    if q == 7:
                        join_rows(i, 1)
                    elif q == 8:
                        negate_maxima(i, 0)
                        negate_maxima(i, 1)
                    dve.wait_ge(panel_done, p + (1 + CREDIT))
                    g = q // 2 if q < 6 else q - 6
                    to = (k_t, q_t)[q % 2][:, g, :] if q < 6 else v_t[:, g % 2, :]
                    bank = order(banks[q % RING_ATT][:, :], g)
                    if q in (1, 3, 5):
                        dve.scalar_tensor_tensor(out=grouped(to, g), in0=bank, scalar=HEAD ** -0.5,
                                                 in1=order(rstd[:, :], g), op0=ALU.mult,
                                                 op1=ALU.mult).then_inc(bank_free, 1)
                    else:
                        dve.tensor_tensor(grouped(to, g), bank, order(rstd[:, :], g), ALU.mult).then_inc(bank_free, 1)
                    for before, what, n in AFTER[q]:
                        if before and first:
                            continue
                        j = i - 1 if before else i
                        if what == "scores":
                            score_pieces(j, n)
                        elif what == "rows" and n == 0:
                            join_rows(j, n)
                        elif what == "turn_v":
                            copy_v(j, n)
                        elif what == "attend":
                            combine(j, n)
                    split(p + RING_ATT, q % RING_ATT)
                    if not first:
                        if q == 5:
                            invert()
                        elif q == 6:
                            normalize()
                        elif q == 7:
                            o_lo_part(i - 1)

            inverse_rms(2)
            take_rstd(2)
            dve.wait_ge(dst_ready, 16)
            pair(0, True)
            with dve.Fori(1, PAIRS) as i:
                steps.enter(i - 1, 6)
                pair(i, False)
                steps.leave(PAIRS - 1)
            last = PAIRS - 1
            copy_v(last, 2)
            for unit in range(4):
                combine(last, unit)
                if unit == 1:
                    split(MLP1 - 1, RING - 1)
            invert()
            normalize()
            o_lo_part(last)
            dve.sem_inc(bank_free, KC // 2)
            for j in range(KC + 1):
                if j < KC:
                    if j % 2 == 0:
                        dve.wait_ge(wo_done, j // 2 + 1)
                    else:
                        dve.wait_ge(panel_done, WO0 + j // 2 + 1 + CREDIT)
                    dve.tensor_tensor(h[:, j, :], h[:, j, :], banks[j][:, :], ALU.add).then_inc(h_ready, 1)
                if j:
                    dve.wait_ge(h_ready, KC + j)
                    normed(xn_hi, xn_lo, GMLP1, j - 1, xhi_done, X_MLP1 + j, xn_ready)
            dve.wait_ge(lo_done, MLP1 + 2 + CREDIT)
            for c in (2, 3):
                ahead(WO0, 0, c)
            mlp(MLP1, Z_MLP1, 3, ())

            inverse_rms(4)
            dve.wait_ge(inv_spread, 5)
            dve.tensor_copy(rstd[:, :], banks[STAT][:, :]).then_inc(rstd_copied, 1)
            dve.wait_ge(rstd_copied, 1)
            for k in FINAL_DVE:
                dve.scalar_tensor_tensor(out=final[:, k, :], in0=h[:, k, :], scalar=cst[:, GFIN + k:GFIN + k + 1],
                                         in1=rstd[:, :], op0=ALU.mult, op1=ALU.mult).then_inc(out_ready, 1)

        @block.gpsimd
        def _(pool):
            pool.memset(ones[:, :], 1.0).then_inc(ones_ready, 1)
            pool.memset(cu[:, 0:2], 0.0).then_inc(ones_ready, 1)
            steps = Steps()

            def squares(n, chunk_ready, chunks=KC, done=sq_ready):
                if n:
                    pool.wait_ge(ss_done, n)
                for k in range(chunks):
                    pool.wait_ge(*chunk_ready(k))
                    if steps.count():
                        pool.wait_ge(sq_step, steps.count())
                    to = sq if k else sq_sum
                    pool.tensor_tensor(to[:, :], h[:, k, :], h[:, k, :], ALU.mult).then_inc(sq_step, steps.add())
                    if k:
                        pool.wait_ge(sq_step, steps.count())
                        ins = pool.tensor_tensor(sq_sum[:, :], sq_sum[:, :], sq[:, :], ALU.add)
                        if k < chunks - 1:
                            ins.then_inc(sq_step, steps.add())
                        else:
                            ins.then_inc(done, 1)

            squares(0, lambda k: (x_ready[k], 16), KC // 2, x_squares)
            squares(1, lambda k: (bank_free, OUT0 + k + 1 + CREDIT))
            squares(2, lambda k: (h_ready, k + 1))
            pool.wait_ge(panel_done, ATT0 + CREDIT)
            pool.memset(v_sb[:, :, :, HEAD:2 * HEAD], 1.0).then_inc(vones_ready, 1)
            for c in range(2):
                pool.wait_ge(hi_done, MLP1 + c + 1)
                pool.tensor_tensor(w_lo[:, c, :], w_raw[:, c, :], w_hi[:, c, :].bitcast(F32),
                                   ALU.subtract).then_inc(lo_done, 1)
            squares(3, lambda k: (h_ready, KC + k + 1))
            squares(4, lambda k: (h_ready, 2 * KC + k + 1), KC - 2)
            for n, k in enumerate(FINAL_POOL):
                pool.tensor_scalar(final[:, k, :], h[:, k, :], cst[:, GFIN + k:GFIN + k + 1], None,
                                   ALU.mult).then_inc(gained, 1)
            pool.wait_ge(gained, len(FINAL_POOL))
            pool.wait_ge(rstd_copied, 1)
            for k in FINAL_POOL:
                pool.tensor_tensor(final[:, k, :], final[:, k, :], rstd[:, :],
                                   ALU.mult).then_inc(pool_out_ready, 1)


def build(nc, arrays):
    ins = {n: nc.dram_tensor(n, a.shape, F32, kind="ExternalInput").ap() for n, a in arrays.items()}
    out_t = nc.dram_tensor("out_t", (KC, P, SEQ), F32, kind="ExternalOutput").ap()
    yoco_trunk(nc, ins["x_t"], ins["weights"], ins["consts"], ins["dist"], ins["ident"], out_t)


def kernel(x, norm_mix, norm_mlp, w_a_in, conv_w, w_a_out, norm_kv, w_kv, w_q, w_o, w_up, w_down, norm_final):
    import numpy as np
    import concourse.bacc as bacc
    from concourse.bass_utils import run_bass_kernel_spmd

    f = np.float32
    x, norm_mix, norm_mlp, w_a_in, conv_w, w_a_out, norm_kv, w_kv, w_q, w_o, w_up, w_down, norm_final = (
        np.asarray(a) for a in (x, norm_mix, norm_mlp, w_a_in, conv_w, w_a_out, norm_kv, w_kv, w_q, w_o,
                                w_up, w_down, norm_final))

    def blocks(w, row, col, rows=D):
        return w[row:row + rows, col:col + P].reshape(rows // P, P, P).transpose(1, 0, 2)

    panels = []
    for j in range(KC):
        panels += [blocks(w_a_in[0], 0, part * D + j * P) for part in (1, 2, 0)]
    panels += [blocks(w_a_out[0], 0, j * P) for j in range(KC)]

    def mlp(layer):
        for half in range(2):
            for j in range(ZC):
                yield blocks(w_up[layer], 0, half * HALF + j * P)
            for j in range(KC):
                for part in range(2):
                    yield blocks(w_down[layer], half * HALF + part * D, j * P)

    panels += mlp(0)
    width = H_G * HEAD
    for pair in range(PAIRS):
        for g in range(N_GROUPS):
            panels += [blocks(w_kv, 0, g * 2 * width + pair * P), blocks(w_q[0], 0, g * width + pair * P)]
        panels += [blocks(w_kv, 0, (g * 2 + 1) * width + pair * P) for g in range(N_GROUPS)]
    for j in range(0, KC, 2):
        panels.append(np.concatenate([blocks(w_o[0], 0, (j + s) * P, width) for s in range(2)], axis=1))
    panels += mlp(1)

    consts = np.zeros((P, N_CONST), f)
    gains = (norm_mix[0], norm_mlp[0], norm_kv, norm_mix[1], norm_mlp[1], norm_final)
    for n, gain in enumerate(gains + tuple(conv_w[0])):
        consts[:, n * KC:(n + 1) * KC] = gain.reshape(KC, P).T
    consts[:, SLOPES:SLOPES + H_G] = [-(2.0 ** -(n + 1)) for n in range(H_G)]
    consts[:, EPSC] = EPS

    a, c = np.arange(P)[:, None], np.arange(P)[None, :]
    own = np.where(c <= a, a - c, MASKED).astype(f)
    prev = np.where(c >= a, P + a - c, MASKED).astype(f)
    group1 = np.where(c <= a, DILATIONS[1] * (a - c), MASKED)
    group2 = np.where(group1 % DILATIONS[2] == 0, group1, MASKED)
    dist = np.concatenate([own, prev, own, prev, own, group1, group2], axis=1).astype(f)

    arrays = {
        "x_t": np.ascontiguousarray(x[0].T.reshape(KC, P, SEQ)),
        "weights": np.stack([p.reshape(P, PANEL) for p in panels]),
        "consts": consts, "dist": dist, "ident": np.eye(P, dtype=f),
    }
    nc = bacc.Bacc("TRN2", target_bir_lowering=False, num_devices=1)
    build(nc, arrays)
    r = run_bass_kernel_spmd(nc, [arrays], core_ids=[0])
    return r.results[0]["out_t"].reshape(D, SEQ).T[None]
```
